# Optimizing a Trainium2 kernel written in Bass

```python
import math
import jax, jax.numpy as jnp
from jax import lax
import numpy as np

D_MODEL = 1024
BATCH = 1
SEQ = 2048
DEPTH = 1
DEC_BATCH = 8
DEC_SEQ = 4
PAST_LEN = 8192
PAGE_SIZE = 128

HEAD_DIM = 64
MIX_WIDTH = D_MODEL
ATTN_SCALE = HEAD_DIM ** -0.5
H_A = MIX_WIDTH // 4 // HEAD_DIM
HKV_A = H_A // 2
WIN_A = 128
H_C = MIX_WIDTH // 4 // HEAD_DIM
HKV_C = H_C
C_BRANCHES = ((128, 1), (512, 4), (2048, 16))
WIN_C_MAX = 2048
D_INNER_B = MIX_WIDTH // 2
SSM_HEAD_DIM = 64
H_B = D_INNER_B // SSM_HEAD_DIM
SSM_GROUPS = 2
D_STATE = 128
CONV_K = 4
CONV_DIM = D_INNER_B + 2 * SSM_GROUPS * D_STATE
SSD_CHUNK = 128
D_FF = 4 * D_MODEL
NUM_BUCKETS = 32
REL_MAX_DIST = 2048
BLOCK = 128
EPS = 1e-6
IN_SPLITS = (H_A * HEAD_DIM, HKV_A * HEAD_DIM, HKV_A * HEAD_DIM,
             H_C * HEAD_DIM, HKV_C * HEAD_DIM, HKV_C * HEAD_DIM,
             D_INNER_B, CONV_DIM, H_B)
IN_COLS = sum(IN_SPLITS)

kernel_name = "hymba_swa_ssd_dilated_decoder_step"

def rms_normalize(x):
    xf = x.astype(jnp.float32)
    return xf * lax.rsqrt(jnp.mean(xf * xf, axis=-1, keepdims=True) + EPS)

def rmsnorm(x, g):
    return (rms_normalize(x) * g.astype(jnp.float32)).astype(x.dtype)

def t5_bucket(dist):
    max_exact = NUM_BUCKETS // 2
    d = jnp.maximum(dist, 0)
    df = jnp.maximum(d, 1).astype(jnp.float32)
    large = max_exact + (jnp.log(df / max_exact) / math.log(REL_MAX_DIST / max_exact)
                         * (NUM_BUCKETS - max_exact)).astype(jnp.int32)
    return jnp.where(d < max_exact, d, jnp.minimum(large, NUM_BUCKETS - 1))

def rel_bias(dist, table):
    return jnp.moveaxis(table[t5_bucket(dist)].astype(jnp.float32), -1, 0)

def softmax_with_sink(logits, valid, sink):
    masked = jnp.where(valid, logits, -jnp.inf)
    m = jnp.max(masked, axis=-1, keepdims=True)
    if sink is not None:
        m = jnp.maximum(m, sink)
    p = jnp.exp(masked - m)
    den = jnp.sum(p, axis=-1, keepdims=True)
    if sink is not None:
        den = den + jnp.exp(sink - m)
    return p / den, (m + jnp.log(den))[..., 0]

def banded_attention(q, k, v, window, dil, table, sink):
    assert window <= BLOCK
    n, L, H, dh = q.shape
    hkv = k.shape[2]
    g = H // hkv
    nb = -(-L // BLOCK)
    lp = nb * BLOCK
    padw = ((0, 0), (0, lp - L), (0, 0), (0, 0))
    qb = jnp.pad(q, padw).astype(jnp.float32).reshape(n, nb, BLOCK, hkv, g, dh)

    def with_prev(x):
        xb = jnp.pad(x, padw).astype(jnp.float32).reshape(n, nb, BLOCK, hkv, dh)
        prev = jnp.pad(xb, ((0, 0), (1, 0), (0, 0), (0, 0), (0, 0)))[:, :nb]
        return jnp.concatenate([prev, xb], axis=2)

    kb = with_prev(k)
    vb = with_prev(v)
    qi = jnp.arange(BLOCK)[:, None]
    kj = jnp.arange(2 * BLOCK)[None, :]
    dist = BLOCK + qi - kj
    kpos = jnp.arange(nb)[:, None, None] * BLOCK - BLOCK + kj
    valid = (dist >= 0) & (dist <= window) & (kpos >= 0)
    bias = rel_bias(dist * dil, table).reshape(hkv, g, BLOCK, 2 * BLOCK)
    logits = jnp.einsum('nbqhgd,nbshd->nbhgqs', qb, kb) + bias
    sk = None if sink is None else sink.astype(jnp.float32).reshape(hkv, g, 1, 1)
    probs, lse = softmax_with_sink(logits, valid[None, :, None, None], sk)
    out = jnp.einsum('nbhgqs,nbshd->nbqhgd', probs, vb).reshape(n, lp, H, dh)[:, :L]
    lse = lse.transpose(0, 1, 4, 2, 3).reshape(n, lp, H)[:, :L]
    return out, lse

def dilated_banded_attention(q, k, v, window, dil, table):
    n, L = q.shape[:2]

    def to_res(x):
        return x.reshape(n, L // dil, dil, *x.shape[2:]).swapaxes(1, 2).reshape(n * dil, L // dil, *x.shape[2:])

    def from_res(x):
        return x.reshape(n, dil, L // dil, *x.shape[2:]).swapaxes(1, 2).reshape(n, L, *x.shape[2:])

    out, lse = banded_attention(to_res(q), to_res(k), to_res(v), window // dil, dil, table, None)
    return from_res(out), from_res(lse)

def gathered_window_attention(q, kbuf, vbuf, knew, vnew, window, dil, table, sink):
    n, T, H, dh = q.shape
    hkv = knew.shape[2]
    g = H // hkv
    kc = jnp.concatenate([kbuf, knew.astype(kbuf.dtype)], axis=1)
    vc = jnp.concatenate([vbuf, vnew.astype(vbuf.dtype)], axis=1)
    lbuf = kbuf.shape[1]
    steps = jnp.arange(window // dil + 1)
    idx = lbuf + jnp.arange(T)[:, None] - steps[None, :] * dil
    valid = idx >= 0
    idx = jnp.maximum(idx, 0)
    kg = kc[:, idx].astype(jnp.float32)
    vg = vc[:, idx].astype(jnp.float32)
    qg = q.astype(jnp.float32).reshape(n, T, hkv, g, dh)
    bias = rel_bias(steps * dil, table).reshape(hkv, g, -1)
    logits = jnp.einsum('nthgd,ntshd->nthgs', qg, kg) + bias
    sk = None if sink is None else sink.astype(jnp.float32).reshape(hkv, g, 1)
    probs, lse = softmax_with_sink(logits, valid[None, :, None, None, :], sk)
    out = jnp.einsum('nthgs,ntshd->nthgd', probs, vg).reshape(n, T, H, dh)
    return out, lse.reshape(n, T, H)

def causal_dwconv(xbc, prev, w, b):
    xpad = jnp.concatenate([prev.astype(xbc.dtype), xbc], axis=1)
    y = lax.conv_general_dilated(xpad, w[:, None, :].astype(xbc.dtype), (1,), 'VALID',
                                 dimension_numbers=('NWC', 'WIO', 'NWC'),
                                 feature_group_count=CONV_DIM)
    return y + b.astype(xbc.dtype), xpad[:, -(CONV_K - 1):]

def ssd_chunked(x, dt, A, Bm, Cm, h0):
    n, L, H, P = x.shape
    f32 = jnp.float32
    rep = H // Bm.shape[2]
    Bh = jnp.repeat(Bm.astype(f32), rep, axis=2)
    Ch = jnp.repeat(Cm.astype(f32), rep, axis=2)
    Q = min(SSD_CHUNK, L)
    nc = -(-L // Q)
    pad = nc * Q - L

    def chunks(t):
        t = jnp.pad(t, ((0, 0), (0, pad)) + ((0, 0),) * (t.ndim - 2))
        return t.reshape(n, nc, Q, *t.shape[2:])

    xc = chunks(x.astype(f32) * dt[..., None])
    ac = chunks(dt * A)
    Bc = chunks(Bh)
    Cc = chunks(Ch)
    acum = jnp.cumsum(ac, axis=2)
    causal = jnp.tril(jnp.ones((Q, Q), dtype=bool))
    seg = acum[:, :, :, None, :] - acum[:, :, None, :, :]
    decay = jnp.exp(jnp.where(causal[None, None, :, :, None], seg, -jnp.inf))
    scores = jnp.einsum('nclhd,ncshd->nclsh', Cc, Bc) * decay
    y_diag = jnp.einsum('nclsh,ncshp->nclhp', scores, xc)
    to_end = jnp.exp(acum[:, :, -1:, :] - acum)
    states = jnp.einsum('nclhd,nclhp->nchpd', Bc * to_end[..., None], xc)
    chunk_decay = jnp.exp(acum[:, :, -1, :])

    def step(h, inp):
        dec, st = inp
        return h * dec[..., None, None] + st, h

    h_last, h_prev = lax.scan(step, h0.astype(f32),
                              (chunk_decay.swapaxes(0, 1), states.swapaxes(0, 1)))
    h_prev = h_prev.swapaxes(0, 1)
    y_off = jnp.einsum('nclhd,nchpd->nclhp', Cc * jnp.exp(acum)[..., None], h_prev)
    y = (y_diag + y_off).reshape(n, nc * Q, H, P)[:, :L]
    return y, h_last

def hybrid_layer(h, W, l, past):
    n, L, _ = h.shape
    f32 = jnp.float32
    u = rmsnorm(h, W['norm_mix_g'][l])
    proj = u @ W['w_in'][l]
    offs = []
    acc = 0
    for s in IN_SPLITS[:-1]:
        acc += s
        offs.append(acc)
    qa, ka, va, qc, kc, vc, z, xbc, dt_raw = jnp.split(proj, offs, axis=-1)
    tab_a = W['rel_bias'][:, :H_A]
    tab_c = W['rel_bias'][:, H_A:]

    qa = rmsnorm(qa.reshape(n, L, H_A, HEAD_DIM), W['a_q_norm_g'][l]) * ATTN_SCALE
    ka = rmsnorm(ka.reshape(n, L, HKV_A, HEAD_DIM), W['a_k_norm_g'][l])
    va = va.reshape(n, L, HKV_A, HEAD_DIM)
    if past is None:
        oa, _ = banded_attention(qa, ka, va, WIN_A, 1, tab_a, W['a_sinks'][l])
    else:
        oa, _ = gathered_window_attention(qa, past[0], past[1], ka, va, WIN_A, 1, tab_a, W['a_sinks'][l])

    qc = rmsnorm(qc.reshape(n, L, H_C, HEAD_DIM), W['c_q_norm_g'][l]) * ATTN_SCALE
    kc = rmsnorm(kc.reshape(n, L, HKV_C, HEAD_DIM), W['c_k_norm_g'][l])
    vc = vc.reshape(n, L, HKV_C, HEAD_DIM)
    outs, lses = [], []
    for window, dil in C_BRANCHES:
        if past is None:
            o, s = dilated_banded_attention(qc, kc, vc, window, dil, tab_c)
        else:
            o, s = gathered_window_attention(qc, past[2], past[3], kc, vc, window, dil, tab_c, None)
        outs.append(o)
        lses.append(s)
    wts = jax.nn.softmax(jnp.stack(lses, axis=-1), axis=-1)
    oc = jnp.einsum('nlhbd,nlhb->nlhd', jnp.stack(outs, axis=-2), wts)

    conv_prev = jnp.zeros((n, CONV_K - 1, CONV_DIM), h.dtype) if past is None else past[5]
    h0 = jnp.zeros((n, H_B, SSM_HEAD_DIM, D_STATE), f32) if past is None else past[4]
    xbc_c, conv_new = causal_dwconv(xbc, conv_prev, W['conv_w'][l], W['conv_b'][l])
    xbc_c = jax.nn.silu(xbc_c)
    xs, bm, cm = jnp.split(xbc_c, [D_INNER_B, D_INNER_B + SSM_GROUPS * D_STATE], axis=-1)
    xs = xs.reshape(n, L, H_B, SSM_HEAD_DIM)
    dt = jax.nn.softplus(dt_raw.astype(f32) + W['dt_bias'][l].astype(f32))
    A = -jnp.exp(W['a_log'][l].astype(f32))
    y, h_last = ssd_chunked(xs, dt, A, bm.reshape(n, L, SSM_GROUPS, D_STATE),
                            cm.reshape(n, L, SSM_GROUPS, D_STATE), h0)
    y = y + W['d_skip'][l].astype(f32)[:, None] * xs.astype(f32)
    gated = (y.reshape(n, L, D_INNER_B) * jax.nn.silu(z.astype(f32))).reshape(n, L, SSM_GROUPS, -1)
    ob = (rms_normalize(gated).reshape(n, L, D_INNER_B) * W['ssm_norm_g'][l].astype(f32)).astype(h.dtype)

    mixed = jnp.concatenate([oa.reshape(n, L, -1).astype(h.dtype), ob,
                             oc.reshape(n, L, -1).astype(h.dtype)], axis=-1)
    h = h + mixed @ W['w_out'][l]

    u2 = rmsnorm(h, W['norm_mlp_g'][l])
    h = h + jnp.square(jax.nn.relu(u2 @ W['w_up'][l])) @ W['w_down'][l]

    if past is None:
        la = min(WIN_A, L)
        lc = min(WIN_C_MAX, L)
        st = (ka[:, L - la:], va[:, L - la:], kc[:, L - lc:], vc[:, L - lc:],
              h_last.astype(h.dtype), conv_new)
    else:
        st = (ka, va, kc, vc, h_last.astype(h.dtype), conv_new)
    return h, st

def run_trunk(x, W, past):
    h = x
    per_layer = []
    for l in range(DEPTH):
        past_l = None if past is None else tuple(c[l] for c in past)
        h, st = hybrid_layer(h, W, l, past_l)
        per_layer.append(st)
    stacked = tuple(jnp.stack([st[i] for st in per_layer]) for i in range(6))
    return h, stacked

def setup_inputs(seed: int = 0) -> dict:
    key = jax.random.key(seed)
    ks = jax.random.split(key, 32)
    f32 = jnp.float32

    def nrm(k, shape, scale):
        return jax.random.normal(k, shape, f32) * scale

    def gain(k, shape):
        return 1.0 + 0.05 * jax.random.normal(k, shape, f32)

    la = min(WIN_A, PAST_LEN)
    lc = min(WIN_C_MAX, PAST_LEN)
    dt0 = jnp.exp(jax.random.uniform(ks[20], (DEPTH, H_B), f32, math.log(1e-3), math.log(1e-1)))
    dt_bias = dt0 + jnp.log(-jnp.expm1(-dt0))
    a_log = jnp.log(jax.random.uniform(ks[21], (DEPTH, H_B), f32, 1.0, 16.0))
    return {
        'x_prompt': nrm(ks[0], (BATCH, SEQ, D_MODEL), 1.0),
        'x_sample': nrm(ks[1], (DEC_BATCH, DEC_SEQ, D_MODEL), 1.0),
        'cache_a_k': nrm(ks[2], (DEPTH, DEC_BATCH, la, HKV_A, HEAD_DIM), 1.0),
        'cache_a_v': nrm(ks[3], (DEPTH, DEC_BATCH, la, HKV_A, HEAD_DIM), 1.0),
        'cache_c_k': nrm(ks[4], (DEPTH, DEC_BATCH, lc, HKV_C, HEAD_DIM), 1.0),
        'cache_c_v': nrm(ks[5], (DEPTH, DEC_BATCH, lc, HKV_C, HEAD_DIM), 1.0),
        'state_ssm': nrm(ks[6], (DEPTH, DEC_BATCH, H_B, SSM_HEAD_DIM, D_STATE), 0.1),
        'state_conv': nrm(ks[7], (DEPTH, DEC_BATCH, CONV_K - 1, CONV_DIM), 1.0),
        'norm_mix_g': gain(ks[8], (DEPTH, D_MODEL)),
        'w_in': nrm(ks[9], (DEPTH, D_MODEL, IN_COLS), D_MODEL ** -0.5),
        'a_q_norm_g': gain(ks[10], (DEPTH, HEAD_DIM)),
        'a_k_norm_g': gain(ks[11], (DEPTH, HEAD_DIM)),
        'a_sinks': nrm(ks[12], (DEPTH, H_A), 0.5),
        'c_q_norm_g': gain(ks[13], (DEPTH, HEAD_DIM)),
        'c_k_norm_g': gain(ks[14], (DEPTH, HEAD_DIM)),
        'rel_bias': nrm(ks[15], (NUM_BUCKETS, H_A + H_C), 0.5),
        'conv_w': nrm(ks[16], (DEPTH, CONV_K, CONV_DIM), CONV_K ** -0.5),
        'conv_b': nrm(ks[17], (DEPTH, CONV_DIM), 0.02),
        'dt_bias': dt_bias,
        'a_log': a_log,
        'd_skip': gain(ks[18], (DEPTH, H_B)),
        'ssm_norm_g': gain(ks[19], (DEPTH, D_INNER_B)),
        'w_out': nrm(ks[22], (DEPTH, MIX_WIDTH, D_MODEL), 0.5 * MIX_WIDTH ** -0.5),
        'norm_mlp_g': gain(ks[23], (DEPTH, D_MODEL)),
        'w_up': nrm(ks[24], (DEPTH, D_MODEL, D_FF), D_MODEL ** -0.5),
        'w_down': nrm(ks[25], (DEPTH, D_FF, D_MODEL), 0.5 * D_FF ** -0.5),
    }

def reference(x_prompt, x_sample, cache_a_k, cache_a_v, cache_c_k, cache_c_v, state_ssm, state_conv,
              norm_mix_g, w_in, a_q_norm_g, a_k_norm_g, a_sinks, c_q_norm_g, c_k_norm_g, rel_bias,
              conv_w, conv_b, dt_bias, a_log, d_skip, ssm_norm_g, w_out, norm_mlp_g, w_up, w_down):
    W = {
        'norm_mix_g': norm_mix_g, 'w_in': w_in,
        'a_q_norm_g': a_q_norm_g, 'a_k_norm_g': a_k_norm_g, 'a_sinks': a_sinks,
        'c_q_norm_g': c_q_norm_g, 'c_k_norm_g': c_k_norm_g, 'rel_bias': rel_bias,
        'conv_w': conv_w, 'conv_b': conv_b, 'dt_bias': dt_bias, 'a_log': a_log,
        'd_skip': d_skip, 'ssm_norm_g': ssm_norm_g, 'w_out': w_out,
        'norm_mlp_g': norm_mlp_g, 'w_up': w_up, 'w_down': w_down,
    }
    y_prompt, st_p = run_trunk(x_prompt, W, None)
    past = (cache_a_k, cache_a_v, cache_c_k, cache_c_v, state_ssm, state_conv)
    y_sample, st_s = run_trunk(x_sample, W, past)
    p_a_k, p_a_v, p_c_k, p_c_v, p_ssm, p_conv = st_p
    s_a_k, s_a_v, s_c_k, s_c_v, s_ssm, s_conv = st_s
    return (y_prompt, y_sample, p_a_k, p_a_v, p_c_k, p_c_v, p_ssm, p_conv,
            s_a_k, s_a_v, s_c_k, s_c_v, s_ssm, s_conv)


_drawn_inputs = setup_inputs


def setup_inputs(seed=0):
    import zlib

    import numpy as np

    out = dict(_drawn_inputs(seed))
    spreads = {}
    factors = {'a_q_norm_g': 23.749,
     'a_sinks': 200.0,
     'c_q_norm_g': 25.134,
     'rel_bias': 2.843,
     'd_skip': 5.497,
     'ssm_norm_g': 3.305,
     'norm_mlp_g': 2.758}
    for name, (base, spread) in spreads.items():
        noise = np.random.default_rng([zlib.crc32(name.encode()), seed]).standard_normal(out[name].shape)
        drawn = base * np.exp(spread * noise) if base else spread * noise
        out[name] = __import__('jax').numpy.asarray(drawn.astype(out[name].dtype))
    for name, factor in factors.items():
        out[name] = (out[name] * factor).astype(out[name].dtype)
    return out
```

```python
from contextlib import ExitStack
import math

import numpy as np

import concourse.bass as bass
from concourse import mybir
from concourse.alu_op_type import AluOpType as ALU

ACT = mybir.ActivationFunctionType
AX = mybir.AxisListType
F32 = mybir.dt.float32
F16 = mybir.dt.float16
BF16 = mybir.dt.bfloat16

P = 128
D = 1024
KT = D // P
SEQ, DEC_N, DEC_T = 2048, 8, 4
NS = DEC_N * DEC_T
TOK = SEQ + NS
NT = SEQ // P
HD = 64
STATE = 128
HB = 8
COLS = 2824
QKV = 1280
ZX = 1536
TC = QKV + HB
FF = 4096
WS = 64.0
HS = 4.0
EPS = 1e-6
NEG = -1e30
DILS = (1, 4, 16)
WIN = 128
LINE = 384
OROW = 264


class Alloc:

    def __init__(self, nc, ctx, stage, before=None):
        self.nc, self.ctx, self.stage, self.before = nc, ctx, stage, before
        self.own = []
        if before is not None:
            ctx.callback(before.release)

    def sb(self, name, shape, dt=F32):
        return self.ctx.enter_context(self.nc.sbuf_tensor(f"{self.stage}_{name}", shape, dt))

    def ps(self, name, shape, dt=F32):
        return self.ctx.enter_context(self.nc.psum_tensor(f"{self.stage}_{name}", shape, dt))

    def sem(self, name):
        self.own.append(self.nc.alloc_semaphore(f"{self.stage}_{name}"))
        return self.own[-1]

    def sems(self, name, n):
        return [self.sem(f"{name}{i}") for i in range(n)]

    def clear_last(self, pool):
        nums = sorted(s.num for s in self.before.own) if self.before is not None else []
        while nums:
            n = 1
            while n < len(nums) and nums[n] == nums[0] + n:
                n += 1
            pool.sem_clear(range(nums[0], nums[0] + n))
            nums = nums[n:]

    def release(self):
        for s in self.own:
            self.nc.release_semaphore(s)


def known_at_least(n, least):
    return not isinstance(n, int) or n >= least


def spread(ap, shape):
    return ap.unsqueeze(len(ap.shape)).to_broadcast(shape)



def project(nc, io, before):
    with ExitStack() as ctx:
        a = Alloc(nc, ctx, "proj", before)
        w_raw = a.sb("w_raw", [P, 2, COLS // 2])
        w_hi = a.sb("w_hi", [P, KT, COLS], F16)
        w_lo = a.sb("w_lo", [P, KT, COLS], F16)
        x = a.sb("x", [P, 4, D])
        junk = a.sb("junk", [P, D], BF16)
        u_hi = a.sb("u_hi", [P, KT, 512], F16)
        u_lo = a.sb("u_lo", [P, KT, 512], F16)
        raw = a.sb("raw", [P, KT, 515])
        raw_s = a.sb("raw_s", [P, KT, DEC_N, 7])
        acc = a.sb("acc", [P, 2, 512])
        col = a.sb("col", [P, 4, 512])
        tok = a.sb("tok", [P, 2, TC])
        sq = a.sb("sq", [P, 14, HD])
        ss = a.sb("ss", [P, 4])
        rr = a.sb("rr", [P, 4])
        hss = a.sb("hss", [P, 2, 14])
        hrr = a.sb("hrr", [P, 2, 14])
        ident = a.sb("ident", [P, P])
        g_mix = a.sb("g_mix", [P, KT])
        cw = a.sb("cw", [P, KT, 4])
        cb = a.sb("cb", [P, KT])
        g_head = a.sb("g_head", [P, 14, HD])
        eps = a.sb("eps", [P, 1])
        turned = [a.ps(f"turned{i}", [P, 512]) for i in range(2)]
        colp = [a.ps(f"colp{i}", [P, 512]) for i in range(2)]
        tokp = [a.ps(f"tokp{i}", [P, 512]) for i in range(4)]

        w_in = a.sems("w_in", 2)
        w_hi_done, w_lo_done = a.sem("w_hi_done"), a.sem("w_lo_done")
        const_in, eps_set, halo_set = a.sem("const_in"), a.sem("eps_set"), a.sem("halo_set")
        x_in = a.sems("x_in", 4)
        squared, logged, rms_ready = a.sem("squared"), a.sem("logged"), a.sem("rms_ready")
        normed, turned_done = a.sem("normed"), a.sem("turned_done")
        hi_done, lo_done = a.sem("hi_done"), a.sem("lo_done")
        col_done, col_taken = a.sem("col_done"), a.sem("col_taken")
        tap, conv_done, halo_done = a.sem("tap"), a.sem("conv_done"), a.sem("halo_done")
        col_ready, col_out = a.sem("col_ready"), a.sems("col_out", 4)
        tok_done, tok_taken = a.sem("tok_done"), a.sem("tok_taken")
        head_sq, head_sum, head_log, head_rms = (a.sem(s) for s in ("head_sq", "head_sum", "head_log", "head_rms"))
        head_scaled, tok_ready, tok_out = a.sem("head_scaled"), a.sem("tok_ready"), a.sems("tok_out", 2)
        conv_out = a.sem("conv_out")
        N_CONST = 8

        w_src = io["w_in"].rearrange("(k p) c -> p k c", p=P)
        half = COLS // 2
        x_rows = io["x"]
        zs_rows, xc_rows = io["zs"], io["xc"]

        def blocks(eng, body):
            body(0, 4, P, True)
            with eng.Fori(1, NT // 4) as b:
                body(b, 4, P, True)
            body(NT // 4, 1, NS, False)

        with nc.Block() as block:
            @block.sync
            def _(sp):
                def load_x(n, tiles, nt):
                    for j in range(tiles):
                        if known_at_least(n, 1):
                            sp.wait_ge(turned_done, KT * n)
                        sp.dma_start(x[0:nt, j, :], x_rows[bass.ds(n * 512 + j * P, nt), :]).then_inc(x_in[j], 16)

                def body(n, tiles, nt, prompt):
                    if known_at_least(n, 1):
                        load_x(n, tiles, nt)
                if True:
                    sp.dma_start(g_mix[:, :], io["norm_mix_g"]).then_inc(const_in, 16)
                    sp.dma_start(ident[:, :], io["ident"]).then_inc(const_in, 16)
                    sp.dma_start(cb[:, :], io["conv_b"]).then_inc(const_in, 16)
                    sp.dma_start(cw[:, :, :], io["conv_w"]).then_inc(const_in, 16)
                    sp.dma_start(g_head[:, 0:4, :], io["a_q_norm_g"].partition_broadcast(P).unsqueeze(1).to_broadcast([P, 4, HD])).then_inc(const_in, 16)
                    sp.dma_start(g_head[:, 4:6, :], io["a_k_norm_g"].partition_broadcast(P).unsqueeze(1).to_broadcast([P, 2, HD])).then_inc(const_in, 16)
                    sp.dma_start(g_head[:, 6:10, :], io["c_q_norm_g"].partition_broadcast(P).unsqueeze(1).to_broadcast([P, 4, HD])).then_inc(const_in, 16)
                    sp.dma_start(g_head[:, 10:14, :], io["c_k_norm_g"].partition_broadcast(P).unsqueeze(1).to_broadcast([P, 4, HD])).then_inc(const_in, 16)
                load_x(0, 4, P)
                for i in range(2 * KT):
                    if i >= 2:
                        sp.wait_ge(w_hi_done, i - 1)
                        sp.wait_ge(w_lo_done, i - 1)
                    sp.dma_start(w_raw[:, i % 2, :], w_src[:, i // 2, (i % 2) * half:(i % 2 + 1) * half]).then_inc(w_in[i % 2], 16)
                sp.dma_start(raw_s[:, :, :, 0:3].rearrange("p k n t -> p (k n) t"), io["state_conv"].rearrange("p k n t -> p (k n) t")).then_inc(conv_out, 16)
                blocks(sp, body)
                sp.wait_ge(conv_done, KT * (NT // 4 + 1))
                sp.dma_start(io["p_conv"], raw[:, :, 0:3]).then_inc(conv_out, 16)
                sp.dma_start(io["s_conv"].rearrange("p k n t -> p (k n) t"), raw_s[:, :, :, 4:7].rearrange("p k n t -> p (k n) t")).then_inc(conv_out, 16)
                sp.wait_ge(conv_out, 48)

            @block.gpsimd
            def _(pool):
                a.clear_last(pool)
                pool.memset(eps[:, :], EPS).then_inc(eps_set, 1)
                pool.memset(raw[:, :, 0:3], 0.0).then_inc(halo_set, 1)
                pool.wait_ge(const_in, 16 * N_CONST)
                pool.tensor_scalar(g_head[:, 0:4, :], g_head[:, 0:4, :], HD ** -0.5, None, ALU.mult).then_inc(eps_set, 1)
                pool.tensor_scalar(g_head[:, 6:10, :], g_head[:, 6:10, :], HD ** -0.5, None, ALU.mult).then_inc(eps_set, 1)
                pool.wait_ge(eps_set, 3)

                def body(n, tiles, nt, prompt):
                    for j in range(tiles):
                        t = 4 * n + j
                        pool.wait_ge(head_scaled, t + 1)
                        pool.tensor_tensor(tok[0:nt, j % 2, 0:384], tok[0:nt, j % 2, 0:384],
                                           g_head[0:nt, 0:6, :].rearrange("p h d -> p (h d)"), ALU.mult)
                        pool.tensor_tensor(tok[0:nt, j % 2, 512:1024], tok[0:nt, j % 2, 512:1024],
                                           g_head[0:nt, 6:14, :].rearrange("p h d -> p (h d)"), ALU.mult).then_inc(tok_ready, 1)
                        pool.wait_ge(tok_ready, t + 1)
                        pool.dma_start(io["tok"][bass.ds(n * 512 + j * P, nt), :], tok[0:nt, j % 2, :]).then_inc(tok_out[j % 2], 16)
                blocks(pool, body)
                pool.wait_ge(tok_out[0], 16 * (NT // 2 + 1))
                pool.wait_ge(tok_out[1], 16 * (NT // 2))

            @block.scalar
            def _(act):
                act.wait_ge(eps_set, 1)
                act.wait_ge(const_in, 16 * N_CONST)

                def head_rms_of(n, j, nt):
                    t = 4 * n + j
                    act.wait_ge(head_sum, t + 1)
                    act.activation(hrr[0:nt, j % 2, :], hss[0:nt, j % 2, :], ACT.Ln, bias=eps[0:nt, :], scale=1.0 / HD).then_inc(head_log, 1)
                    act.wait_ge(head_log, t + 1)
                    act.activation(hrr[0:nt, j % 2, :], hrr[0:nt, j % 2, :], ACT.Exp, scale=-0.5).then_inc(head_rms, 1)

                def rms(n, tiles, nt):
                    for j in range(tiles):
                        act.wait_ge(x_in[j], 16 * n + 16)
                        if known_at_least(n, 1):
                            act.wait_ge(normed, 4 * n)
                        if known_at_least(n, 1) or j >= 1:
                            act.wait_ge(squared, 4 * n + j)
                        act.activation(junk[0:nt, :], x[0:nt, j, :], ACT.Square, accum_out=ss[0:nt, j:j + 1]).then_inc(squared, 1)
                    act.wait_ge(squared, 4 * n + tiles)
                    act.activation(ss[0:nt, 0:tiles], ss[0:nt, 0:tiles], ACT.Ln, bias=eps[0:nt, :], scale=1.0 / D).then_inc(logged, 1)
                    act.wait_ge(logged, n + 1)
                    act.activation(rr[0:nt, 0:tiles], ss[0:nt, 0:tiles], ACT.Exp, scale=-0.5).then_inc(rms_ready, 1)

                def store(n, s, w):
                    act.wait_ge(col_ready, 12 * n + s + 1)
                    rows = zs_rows if s < 4 else xc_rows
                    r = s if s < 4 else s - 4
                    act.dma_start(rows[r * P:(r + 1) * P, bass.ds(n * 512, w)], col[:, s % 4, 0:w]).then_inc(col_out[s % 4], 16)

                def body(n, tiles, nt, prompt):
                    w = tiles * nt
                    if known_at_least(n, 1):
                        rms(n, tiles, nt)
                    for k in range(KT):
                        act.wait_ge(turned_done, KT * n + k + 1)
                        act.activation(u_hi[:, k, 0:w], turned[k % 2][:, 0:w], ACT.Copy, scale=g_mix[:, k:k + 1]).then_inc(hi_done, 1)

                    def silu_of(c):
                        act.wait_ge(conv_done, KT * n + c + 1)
                        s = 4 + c
                        if known_at_least(n, 1) or s >= 4:
                            act.wait_ge(col_out[s % 4], 16 * (3 * n + s // 4))
                        act.activation(col[:, s % 4, 0:w], acc[:, c % 2, 0:w], ACT.Silu).then_inc(col_ready, 1)
                        store(n, s - 1, w)

                    for c in range(12):
                        act.wait_ge(col_done, 12 * n + c + 1)
                        if c < 4:
                            if known_at_least(n, 1):
                                act.wait_ge(col_out[c % 4], 16 * 3 * n)
                            act.activation(col[:, c, 0:w], colp[c % 2][:, 0:w], ACT.Silu, scale=1.0 / WS).then_inc(col_ready, 1)
                            if c >= 1:
                                store(n, c - 1, w)
                            continue
                        k = c - 4
                        if prompt:
                            if known_at_least(n, 1):
                                act.wait_ge(conv_done, KT * (n - 1) + k + 1)
                            act.activation(raw[:, k, 3:3 + w], colp[c % 2][:, 0:w], ACT.Copy, scale=1.0 / WS).then_inc(col_taken, 1)
                        else:
                            act.activation(raw_s[:, k, :, 3:7], colp[c % 2][:, 0:w].rearrange("p (n t) -> p n t", t=DEC_T),
                                           ACT.Copy, scale=1.0 / WS).then_inc(col_taken, 1)
                        if k >= 2:
                            silu_of(k - 2)
                    silu_of(6)
                    silu_of(7)
                    store(n, 11, w)
                    for j in range(tiles):
                        for q in range(3):
                            t = 3 * (4 * n + j) + q
                            qw = 512 if q < 2 else TC - 1024
                            act.wait_ge(tok_done, t + 1)
                            if q == 0 and (known_at_least(n, 1) or j >= 2):
                                act.wait_ge(tok_out[j % 2], 16 * (2 * n + j // 2))
                            act.activation(tok[0:nt, j % 2, q * 512:q * 512 + qw], tokp[(3 * j + q) % 4][0:nt, 0:qw],
                                           ACT.Copy, scale=1.0 / WS).then_inc(tok_taken, 1)
                        if j >= 1:
                            head_rms_of(n, j - 1, nt)
                    head_rms_of(n, tiles - 1, nt)

                rms(0, 4, P)
                for i in range(2 * KT):
                    act.wait_ge(w_in[i % 2], 16 * (i // 2 + 1))
                    act.activation(w_hi[:, i // 2, (i % 2) * half:(i % 2 + 1) * half], w_raw[:, i % 2, :], ACT.Copy, scale=WS).then_inc(w_hi_done, 1)
                blocks(act, body)
                for s in range(4):
                    act.wait_ge(col_out[s], 16 * 3 * (NT // 4 + 1))

            @block.vector
            def _(dve):
                dve.wait_ge(const_in, 16 * N_CONST)

                def norm(n, tiles, nt):
                    dve.wait_ge(rms_ready, n + 1)
                    for j in range(tiles):
                        dve.tensor_scalar(x[0:nt, j, :], x[0:nt, j, :], rr[0:nt, j:j + 1], None, ALU.mult).then_inc(normed, 1)

                def body(n, tiles, nt, prompt):
                    w = tiles * nt
                    if known_at_least(n, 1):
                        norm(n, tiles, nt)
                    for k in range(KT):
                        dve.wait_ge(hi_done, KT * n + k + 1)
                        dve.scalar_tensor_tensor(u_lo[:, k, 0:w], turned[k % 2][:, 0:w], g_mix[:, k:k + 1], u_hi[:, k, 0:w],
                                                 ALU.mult, ALU.subtract).then_inc(lo_done, 1)
                    for k in range(KT):
                        dve.wait_ge(col_taken, KT * n + k + 1)
                        if k >= 2 or known_at_least(n, 1):
                            dve.wait_ge(col_ready, 12 * n + 4 + k - 2 + 1 if k >= 2 else 12 * n)
                        if prompt:
                            src = [raw[:, k, i:i + w] for i in range(4)]
                            dst = acc[:, k % 2, 0:w]
                        else:
                            src = [raw_s[:, k, :, i:i + DEC_T] for i in range(4)]
                            dst = acc[:, k % 2, 0:w].rearrange("p (n t) -> p n t", t=DEC_T)
                        if not prompt and k == 0:
                            dve.wait_ge(conv_out, 16)
                        if prompt and not known_at_least(n, 1) and k == 0:
                            dve.wait_ge(halo_set, 1)
                        t = 3 * (KT * n + k)
                        dve.tensor_scalar(dst, src[3], cw[:, k, 3:4], cb[:, k:k + 1], ALU.mult, ALU.add).then_inc(tap, 1)
                        for i in range(2):
                            dve.wait_ge(tap, t + i + 1)
                            dve.scalar_tensor_tensor(dst, src[i], cw[:, k, i:i + 1], dst, ALU.mult, ALU.add).then_inc(tap, 1)
                        dve.wait_ge(tap, t + 3)
                        last = dve.scalar_tensor_tensor(dst, src[2], cw[:, k, 2:3], dst, ALU.mult, ALU.add)
                        if prompt:
                            last.then_inc(halo_done, 1)
                            dve.wait_ge(halo_done, KT * n + k + 1)
                            dve.tensor_copy(raw[:, k, 0:3], raw[:, k, w:w + 3]).then_inc(conv_done, 1)
                        else:
                            last.then_inc(conv_done, 1)

                    def head_sums(j):
                        t = 4 * n + j
                        dve.wait_ge(tok_taken, 3 * t + 2)
                        if known_at_least(n, 1) or j >= 1:
                            dve.wait_ge(head_sum, t)
                        dve.tensor_tensor(sq[0:nt, 0:6, :].rearrange("p h d -> p (h d)"), tok[0:nt, j % 2, 0:384], tok[0:nt, j % 2, 0:384], ALU.mult)
                        dve.tensor_tensor(sq[0:nt, 6:14, :].rearrange("p h d -> p (h d)"), tok[0:nt, j % 2, 512:1024], tok[0:nt, j % 2, 512:1024],
                                          ALU.mult).then_inc(head_sq, 1)
                        dve.wait_ge(head_sq, t + 1)
                        dve.tensor_reduce(hss[0:nt, j % 2, :], sq[0:nt, :, :], AX.X, ALU.add).then_inc(head_sum, 1)

                    def head_scale(j):
                        t = 4 * n + j
                        dve.wait_ge(head_rms, t + 1)
                        for c0, h0, nh in ((0, 0, 6), (512, 6, 8)):
                            v = tok[0:nt, j % 2, c0:c0 + nh * HD].rearrange("p (h d) -> p h d", d=HD)
                            last = dve.tensor_tensor(v, v, spread(hrr[0:nt, j % 2, h0:h0 + nh], [nt, nh, HD]), ALU.mult)
                        last.then_inc(head_scaled, 1)

                    for j in range(tiles):
                        head_sums(j)
                        if j >= 1:
                            head_scale(j - 1)
                    head_scale(tiles - 1)

                norm(0, 4, P)
                for i in range(2 * KT):
                    dve.wait_ge(w_hi_done, i + 1)
                    c = slice((i % 2) * half, (i % 2 + 1) * half)
                    dve.scalar_tensor_tensor(w_lo[:, i // 2, c], w_raw[:, i % 2, :], WS, w_hi[:, i // 2, c], ALU.mult, ALU.subtract).then_inc(w_lo_done, 1)
                blocks(dve, body)

            @block.tensor
            def _(pe):
                pe.wait_ge(const_in, 16 * N_CONST)

                def product(out, k, w_cols, rhs_cols, first, last, w_moves):
                    for i, (w, u) in enumerate(((w_hi, u_hi), (w_hi, u_lo), (w_lo, u_hi))):
                        l, r = w[:, k, w_cols], u[:, k, rhs_cols]
                        if w_moves:
                            l, r = r, l
                        ins = pe.matmul(out, l, r, start=first and i == 0, stop=last and i == 2)
                    return ins

                def body(n, tiles, nt, prompt):
                    w = tiles * nt
                    for k in range(KT):
                        for j in range(tiles):
                            if k == 0:
                                pe.wait_ge(normed, 4 * n + j + 1)
                            if j == 0 and (known_at_least(n, 1) or k >= 2):
                                pe.wait_ge(lo_done, KT * n + k - 1)
                            last = pe.transpose(turned[k % 2][:, j * nt:(j + 1) * nt], x[0:nt, j, k * P:(k + 1) * P], ident[0:nt, 0:nt])
                        last.then_inc(turned_done, 1)
                    for c in range(12):
                        if c in (0, 1) and known_at_least(n, 1):
                            pe.wait_ge(col_taken, KT * n - 1 + c)
                        elif 2 <= c < 6:
                            pe.wait_ge(col_ready, 12 * n + c - 1)
                        elif c >= 6:
                            pe.wait_ge(col_taken, KT * n + c - 5)
                        for k in range(KT):
                            if c == 0:
                                pe.wait_ge(lo_done, KT * n + k + 1)
                                if not known_at_least(n, 1):
                                    pe.wait_ge(w_lo_done, 2 * k + 2)
                            ins = product(colp[c % 2][:, 0:w], k, slice(QKV + c * P, QKV + (c + 1) * P), slice(0, w), k == 0, k == KT - 1, False)
                        ins.then_inc(col_done, 1)
                    for j in range(tiles):
                        for q in range(3):
                            t = 3 * (4 * n + j) + q
                            if known_at_least(n, 1) or 3 * j + q >= 4:
                                pe.wait_ge(tok_taken, t - 3)
                            bank = tokp[(3 * j + q) % 4]
                            parts = [(0, 512, q * 512)] if q < 2 else [(0, 256, 1024), (256, HB, QKV + ZX)]
                            for o, cw_, c0 in parts:
                                for k in range(KT):
                                    ins = product(bank[0:nt, o:o + cw_], k, slice(c0, c0 + cw_), slice(j * nt, (j + 1) * nt), k == 0, k == KT - 1, True)
                            ins.then_inc(tok_done, 1)
                blocks(pe, body)
    return a




def scan(nc, io, before):
    with ExitStack() as ctx:
        a = Alloc(nc, ctx, "scan", before)
        NC = NT + 1
        A_, NACUM, DT, DT_END, DECAY = range(5)
        ident = a.sb("ident", [P, P])
        upper = a.sb("upper", [P, P])
        upper_s = a.sb("upper_s", [NS, NS])
        same_s = a.sb("same_s", [NS, NS])
        of_seq = a.sb("of_seq", [NS, DEC_N])
        ones = a.sb("ones", [P, P])
        eps = a.sb("eps", [P, 1])
        d_skip = a.sb("d_skip", [P, 4])
        g_ssm = a.sb("g_ssm", [P, 4])
        bias = a.sb("bias", [P, HB])
        rate = a.sb("rate", [P, HB])
        dt_x = a.sb("dt_x", [P, NC, HB])
        dt_e = a.sb("dt_e", [P, NC, HB])
        dt_y = a.sb("dt_y", [P, NC, HB])
        dt_l = a.sb("dt_l", [P, NC, HB])
        small = a.sb("small", [P, NC, 5, HB])
        a_seq = a.sb("a_seq", [NS, DEC_N, HB])
        decay_s = a.sb("decay_s", [P, DEC_N, HB])
        state_s = a.sb("state_s", [P, DEC_N, 512])
        xte_s = a.sb("xte_s", [NS, 2, 512])
        cur = a.sb("cur", [P, 2, 5, HB])
        xbc = a.sb("xbc", [P, 2, KT, P])
        zs = a.sb("zs", [P, 2, 4, P])
        b_tok = a.sb("b_tok", [P, 2, 2, P])
        xdt = a.sb("xdt", [P, 2, 512])
        xte = a.sb("xte", [P, 2, 512])
        cb_low = a.sb("cb_low", [P, 2, 2, P])
        dec = a.sb("dec", [P, 2, HB, P])
        grown = a.sb("grown", [P, 2, HB, P])
        mix = a.sb("mix", [P, 2, HB, P])
        c_dec = a.sb("c_dec", [P, 2, HB, P])
        state = a.sb("state", [P, 2, 512])
        y = a.sb("y", [P, 2, 4, P])
        ysq = a.sb("ysq", [P, 2, 4, P])
        rs = a.sb("rs", [P, 2, 2, P])
        m = a.sb("m", [P, 2, 4, P])
        m_hi = a.sb("m_hi", [P, 2, 4, P], F16)
        m_lo = a.sb("m_lo", [P, 2, 4, P], F16)
        psX, psB, psS = a.ps("psX", [P, 4, P]), a.ps("psB", [P, 2, P]), a.ps("psS", [P, 2, P])
        psD = [a.ps(f"psD{i}", [P, 4, P]) for i in range(2)]
        psY, psH, psG = a.ps("psY", [P, 4, P]), a.ps("psH", [P, 512]), a.ps("psG", [P, 4, P])

        const_in, made, dt_in, dt_step = a.sem("const_in"), a.sem("made"), a.sem("dt_in"), a.sem("dt_step")
        dt_act, dt_sum, small_ready = a.sem("dt_act"), a.sem("dt_sum"), a.sem("small_ready")
        chunk_in = a.sems("chunk_in", 2)
        cur_ready, x_turned, b_turned, s_done, d_done = (a.sem(s) for s in ("cur_ready", "x_turned", "b_turned", "s_done", "d_done"))
        b_ready, x_ready, low_ready, grown_ready, seg_ready, dec_ready, mix_ready, c_ready = (
            a.sem(s) for s in ("b_ready", "x_ready", "low_ready", "grown_ready", "seg_ready", "dec_ready", "mix_ready", "c_ready"))
        y_done, h_done, faded, state_ready = (a.sem(s) for s in ("y_done", "h_done", "faded", "state_ready"))
        skipped, gated, sq_ready, g_done, g_log, rs_ready = (a.sem(s) for s in ("skipped", "gated", "sq_ready", "g_done", "g_log", "rs_ready"))
        m_ready, hi_ready, lo_ready = a.sem("m_ready"), a.sem("hi_ready"), a.sem("lo_ready")
        mix_out = a.sems("mix_out", 2)
        s_state_in, picked, hs_done, s_faded, s_state_ready, state_out = (
            a.sem(s) for s in ("s_state_in", "picked", "hs_done", "s_faded", "s_state_ready", "state_out"))
        N_CONST = 9
        tiles_of = io["xc"].rearrange("(k p) t -> p k t", p=P)
        z_of = io["zs"].rearrange("(k p) t -> p k t", p=P)
        hi_of = io["mix_hi"][256:768, :].rearrange("(k p) t -> p k t", p=P)
        lo_of = io["mix_lo"][256:768, :].rearrange("(k p) t -> p k t", p=P)

        def chunks(eng, first, second, third):
            def pair(c):
                for f in (first, second, third):
                    for u in range(2):
                        f(c + u, u, P)
            pair(0)
            with eng.Fori(1, NT // 2) as i:
                pair(2 * i)
            for f in (first, second, third):
                f(NT, 0, NS)

        def past(n):
            return known_at_least(n, 2)

        with nc.Block() as block:
            @block.sync
            def _(sp):
                for dst, src in ((ident, "ident"), (upper, "upper"), (upper_s, "upper_s"), (same_s, "same_s"), (of_seq, "of_seq"),
                                 (d_skip, "d_skip"), (g_ssm, "ssm_norm_g")):
                    sp.dma_start(dst[:, :], io[src]).then_inc(const_in, 16)
                sp.dma_start(bias[:, :], io["dt_bias"].partition_broadcast(P)).then_inc(const_in, 16)
                sp.dma_start(rate[:, :], io["a_log"].partition_broadcast(P)).then_inc(const_in, 16)
                sp.wait_ge(made, 1)
                sp.dma_start(dt_x[:, 0:NT, :], io["tok"][0:SEQ, QKV:TC].rearrange("(c p) h -> p c h", p=P)).then_inc(dt_in, 16)
                sp.dma_start(dt_x[0:NS, NT, :], io["tok"][SEQ:TOK, QKV:TC]).then_inc(dt_in, 16)
                sp.dma_start(state_s[:, :, :], io["state_ssm"]).then_inc(s_state_in, 16)

                def load(c, u, nt):
                    if past(c):
                        sp.wait_ge(gated, c - 1)
                        sp.wait_ge(y_done, c - 1)
                    cols = bass.ds(c * P, nt)
                    sp.dma_start(xbc[:, u, :, 0:nt], tiles_of[:, :, cols]).then_inc(chunk_in[u], 16)
                    sp.dma_start(zs[:, u, :, 0:nt], z_of[:, :, cols]).then_inc(chunk_in[u], 16)

                def store(c, u, nt):
                    cols = bass.ds(c * P, nt)
                    sp.wait_ge(hi_ready, c + 1)
                    sp.dma_start(hi_of[:, :, cols], m_hi[:, u, :, 0:nt]).then_inc(mix_out[u], 16)
                    sp.wait_ge(lo_ready, c + 1)
                    sp.dma_start(lo_of[:, :, cols], m_lo[:, u, :, 0:nt]).then_inc(mix_out[u], 16)
                chunks(sp, load, lambda c, u, nt: None, store)
                sp.wait_ge(state_ready, NT)
                sp.dma_start(io["p_ssm"], state[:, NT % 2, :]).then_inc(state_out, 16)
                sp.wait_ge(s_state_ready, DEC_N)
                sp.dma_start(io["s_ssm"], state_s[:, :, :]).then_inc(state_out, 16)
                sp.wait_ge(state_out, 32)
                sp.wait_ge(mix_out[0], 32 * (NT // 2 + 1))
                sp.wait_ge(mix_out[1], 32 * (NT // 2))

            @block.gpsimd
            def _(pool):
                a.clear_last(pool)
                pool.memset(dt_x[:, :, :], 0.0).then_inc(made, 1)
                pool.memset(ones[:, :], 1.0).then_inc(made, 1)
                pool.memset(eps[:, :], EPS).then_inc(made, 1)

                def grow_c(c, u, nt):
                    pool.wait_ge(grown_ready, c + 1)
                    if past(c):
                        pool.wait_ge(y_done, c - 1)
                    for g in range(2):
                        last = pool.tensor_tensor(c_dec[:, u, 4 * g:4 * g + 4, 0:nt],
                                                  xbc[:, u, 6 + g, 0:nt].unsqueeze(1).to_broadcast([P, 4, nt]),
                                                  grown[:, u, 4 * g:4 * g + 4, 0:nt], ALU.mult)
                    last.then_inc(c_ready, 1)

                def gate(c, u, nt):
                    pool.wait_ge(skipped, c + 1)
                    pool.tensor_tensor(y[:, u, :, 0:nt], y[:, u, :, 0:nt], zs[:, u, :, 0:nt], ALU.mult).then_inc(gated, 1)
                chunks(pool, grow_c, gate, lambda c, u, nt: None)

            @block.scalar
            def _(act):
                act.wait_ge(const_in, 16 * N_CONST)
                act.wait_ge(made, 3)
                act.activation(rate[:, :], rate[:, :], ACT.Exp).then_inc(dt_act, 1)
                act.wait_ge(dt_step, 3)
                act.activation(dt_e[:, :, :], dt_e[:, :, :], ACT.Exp, scale=-1.0).then_inc(dt_act, 1)
                act.wait_ge(dt_step, 4)
                act.activation(dt_l[:, :, :], dt_y[:, :, :], ACT.Ln).then_inc(dt_act, 1)
                act.wait_ge(dt_sum, 3)
                act.activation(small[:, 0:NT, DECAY, :], psH[:, 128:256].rearrange("p (c h) -> p c h", h=HB), ACT.Exp).then_inc(dt_act, 1)
                act.activation(decay_s[:, :, :], psH[:, 320:384].rearrange("p (c h) -> p c h", h=HB), ACT.Exp).then_inc(dt_act, 1)
                act.wait_ge(dt_step, 11)
                act.activation(dt_e[:, :, :], dt_e[:, :, :], ACT.Exp).then_inc(dt_act, 1)

                def first(c, u, nt):
                    if past(c):
                        act.wait_ge(h_done, c - 1)
                    act.wait_ge(b_turned, c + 1)
                    act.activation(b_tok[0:nt, u, :, :], psB[0:nt, :, :], ACT.Copy).then_inc(b_ready, 1)
                    if past(c):
                        act.wait_ge(c_ready, c - 1)
                    act.wait_ge(d_done, c + 1)
                    for i in range(2):
                        last = act.activation(grown[:, u, 4 * i:4 * i + 4, 0:nt], psD[i][:, :, 0:nt], ACT.Exp)
                    last.then_inc(grown_ready, 1)
                    act.wait_ge(seg_ready, c + 1)
                    act.activation(dec[0:nt, u, :, 0:nt], dec[0:nt, u, :, 0:nt], ACT.Exp).then_inc(dec_ready, 1)

                def second(c, u, nt):
                    act.wait_ge(gated, c + 1)
                    if past(c):
                        act.wait_ge(g_done, c - 1)
                    act.activation(ysq[:, u, :, 0:nt], y[:, u, :, 0:nt], ACT.Square).then_inc(sq_ready, 1)

                def third(c, u, nt):
                    act.wait_ge(g_done, c + 1)
                    if past(c):
                        act.wait_ge(m_ready, c - 1)
                    act.activation(rs[:, u, :, 0:nt], psG[:, 0:2, 0:nt], ACT.Ln, bias=eps[:, :], scale=1.0 / 256).then_inc(g_log, 1)
                    act.wait_ge(g_log, c + 1)
                    act.activation(rs[:, u, :, 0:nt], rs[:, u, :, 0:nt], ACT.Exp, scale=-0.5).then_inc(rs_ready, 1)
                    act.wait_ge(m_ready, c + 1)
                    if past(c):
                        act.wait_ge(mix_out[u], 32 * (c // 2) if isinstance(c, int) else 16 * (c - u))
                    act.activation(m_hi[:, u, :, 0:nt], m[:, u, :, 0:nt], ACT.Copy).then_inc(hi_ready, 1)
                chunks(act, first, second, third)

            @block.vector
            def _(dve):
                dve.wait_ge(const_in, 16 * N_CONST)
                dve.wait_ge(dt_in, 32)
                shape = [P, NC, HB]
                step = [0]

                def then(ins):
                    step[0] += 1
                    ins.then_inc(dt_step, 1)
                    dve.wait_ge(dt_step, step[0])

                then(dve.tensor_tensor(dt_x[:, :, :], dt_x[:, :, :], bias[:, :].unsqueeze(1).to_broadcast(shape), ALU.add))
                then(dve.tensor_scalar(dt_e[:, :, :], dt_x[:, :, :], -1.0, None, ALU.mult))
                then(dve.tensor_tensor(dt_e[:, :, :], dt_e[:, :, :], dt_x[:, :, :], ALU.max))
                dve.wait_ge(dt_act, 2)
                then(dve.tensor_scalar(dt_y[:, :, :], dt_e[:, :, :], 1.0, None, ALU.add))
                dve.wait_ge(dt_act, 3)
                then(dve.scalar_tensor_tensor(dt_y[:, :, :], dt_y[:, :, :], -1.0, dt_e[:, :, :], ALU.add, ALU.subtract))
                then(dve.tensor_tensor(dt_l[:, :, :], dt_l[:, :, :], dt_y[:, :, :], ALU.subtract))
                then(dve.scalar_tensor_tensor(small[:, :, DT, :], dt_x[:, :, :], 0.0, dt_l[:, :, :], ALU.max, ALU.add))
                then(dve.scalar_tensor_tensor(small[:, :, A_, :], small[:, :, DT, :], -1.0, rate[:, :].unsqueeze(1).to_broadcast(shape),
                                              ALU.mult, ALU.mult))
                then(dve.tensor_tensor(a_seq[:, :, :], spread(of_seq[:, :], [NS, DEC_N, HB]),
                                       small[0:NS, NT, A_, :].unsqueeze(1).to_broadcast([NS, DEC_N, HB]), ALU.mult))
                dve.wait_ge(dt_sum, 3)
                dve.wait_ge(dt_act, 5)
                dve.memset(small[:, NT, NACUM, :], 0.0)
                then(dve.memset(dt_e[:, NT, :], 0.0))
                dve.tensor_scalar(small[:, 0:NT, NACUM, :], psH[:, 0:128].rearrange("p (c h) -> p c h", h=HB), -1.0, None, ALU.mult)
                dve.tensor_scalar(small[0:NS, NT, NACUM, :], psH[0:NS, 256:264], -1.0, None, ALU.mult)
                dve.memset(small[:, NT, DECAY, :], 0.0).then_inc(made, 1)
                dve.wait_ge(made, 4)
                dve.tensor_tensor(dt_e[0:NS, NT, :], psH[0:NS, 264:272], small[0:NS, NT, NACUM, :], ALU.add)
                then(dve.tensor_tensor(dt_e[:, 0:NT, :], psH[:, 128:256].rearrange("p (c h) -> p c h", h=HB), small[:, 0:NT, NACUM, :], ALU.add))
                dve.wait_ge(dt_act, 6)
                dve.memset(state[:, 0, :], 0.0)
                then(dve.tensor_tensor(small[:, :, DT_END, :], dt_e[:, :, :], small[:, :, DT, :], ALU.mult))

                def first(c, u, nt):
                    if past(c):
                        dve.wait_ge(h_done, c - 1)
                    dve.tensor_copy(cur[:, u, :, :], small[:, bass.ds(c, 1), :, :].rearrange("p o s h -> p (o s) h")).then_inc(cur_ready, 1)
                    dve.wait_ge(cur_ready, c + 1)
                    dve.wait_ge(x_turned, c + 1)
                    xv = psX[0:nt, :, :].rearrange("p k (h d) -> p (k h) d", d=HD)
                    dve.tensor_tensor(xdt[0:nt, u, :].rearrange("p (h d) -> p h d", d=HD), xv, spread(cur[0:nt, u, DT, :], [nt, HB, HD]), ALU.mult)
                    dve.tensor_tensor(xte[0:nt, u, :].rearrange("p (h d) -> p h d", d=HD), xv, spread(cur[0:nt, u, DT_END, :], [nt, HB, HD]),
                                      ALU.mult).then_inc(x_ready, 1)
                    if past(c):
                        dve.wait_ge(mix_ready, c - 1)
                    low = (upper if nt == P else upper_s)[0:nt, 0:nt]
                    dve.wait_ge(s_done, c + 1)
                    dve.tensor_tensor(cb_low[0:nt, u, :, 0:nt], psS[0:nt, :, 0:nt], low.unsqueeze(1).to_broadcast([nt, 2, nt]), ALU.mult).then_inc(low_ready, 1)
                    dve.wait_ge(grown_ready, c + 1)
                    for h in range(HB):
                        last = dve.tensor_scalar(dec[0:nt, u, h, 0:nt], psD[h // 4][0:nt, h % 4, 0:nt], cur[0:nt, u, NACUM, h:h + 1], 0.0, ALU.add, ALU.min)
                    last.then_inc(seg_ready, 1)
                    dve.wait_ge(low_ready, c + 1)
                    dve.wait_ge(dec_ready, c + 1)
                    for g in range(2):
                        last = dve.tensor_tensor(mix[0:nt, u, 4 * g:4 * g + 4, 0:nt], cb_low[0:nt, u, g, 0:nt].unsqueeze(1).to_broadcast([nt, 4, nt]),
                                                 dec[0:nt, u, 4 * g:4 * g + 4, 0:nt], ALU.mult)
                    last.then_inc(mix_ready, 1)

                def second(c, u, nt):
                    if nt == P:
                        if known_at_least(c, 1):
                            dve.wait_ge(y_done, c)
                            dve.wait_ge(state_ready, c)
                        dve.tensor_tensor(state[:, 1 - u, :].rearrange("p (h d) -> p h d", d=HD), state[:, u, :].rearrange("p (h d) -> p h d", d=HD),
                                          spread(cur[:, u, DECAY, :], [P, HB, HD]), ALU.mult).then_inc(faded, 1)
                        dve.wait_ge(faded, c + 1)
                        dve.wait_ge(h_done, c + 1)
                        dve.tensor_tensor(state[:, 1 - u, :], state[:, 1 - u, :], psH[:, :], ALU.add).then_inc(state_ready, 1)
                    else:
                        for n in range(DEC_N):
                            if n >= 2:
                                dve.wait_ge(hs_done, n - 1)
                            dve.tensor_scalar(xte_s[:, n % 2, :], xte[0:NS, u, :], of_seq[:, n:n + 1], None, ALU.mult).then_inc(picked, 1)
                            if n == 0:
                                dve.wait_ge(y_done, c + 1)
                            dve.tensor_tensor(state_s[:, n, :].rearrange("p (h d) -> p h d", d=HD), state_s[:, n, :].rearrange("p (h d) -> p h d", d=HD),
                                              spread(decay_s[:, n, :], [P, HB, HD]), ALU.mult).then_inc(s_faded, 1)
                            dve.wait_ge(s_faded, n + 1)
                            dve.wait_ge(hs_done, n + 1)
                            dve.tensor_tensor(state_s[:, n, :], state_s[:, n, :], psH[:, :], ALU.add).then_inc(s_state_ready, 1)
                    dve.wait_ge(y_done, c + 1)
                    if past(c):
                        dve.wait_ge(m_ready, c - 1)
                    for k in range(4):
                        last = dve.scalar_tensor_tensor(y[:, u, k, 0:nt], xbc[:, u, k, 0:nt], d_skip[:, k:k + 1], psY[:, k, 0:nt], ALU.mult, ALU.add)
                    last.then_inc(skipped, 1)

                def third(c, u, nt):
                    dve.wait_ge(rs_ready, c + 1)
                    if past(c):
                        dve.wait_ge(lo_ready, c - 1)
                    for k in range(4):
                        last = dve.scalar_tensor_tensor(m[:, u, k, 0:nt], y[:, u, k, 0:nt], g_ssm[:, k:k + 1], rs[:, u, k // 2, 0:nt], ALU.mult, ALU.mult)
                    last.then_inc(m_ready, 1)
                    dve.wait_ge(hi_ready, c + 1)
                    dve.tensor_tensor(m_lo[:, u, :, 0:nt], m[:, u, :, 0:nt], m_hi[:, u, :, 0:nt], ALU.subtract).then_inc(lo_ready, 1)
                chunks(dve, first, second, third)

            @block.tensor
            def _(pe):
                pe.wait_ge(const_in, 16 * N_CONST)
                pe.wait_ge(made, 3)
                pe.wait_ge(dt_step, 9)
                av = small[:, 0:NT, A_, :]
                pe.matmul(psH[:, 0:128], upper[:, :], av, start=True, stop=True)
                pe.matmul(psH[:, 128:256], ones[:, :], av, start=True, stop=True).then_inc(dt_sum, 1)
                pe.matmul(psH[0:NS, 256:264], upper_s[:, :], small[0:NS, NT, A_, :], start=True, stop=True)
                pe.matmul(psH[0:NS, 264:272], same_s[:, :], small[0:NS, NT, A_, :], start=True, stop=True).then_inc(dt_sum, 1)
                pe.matmul(psH[:, 320:384], ones[0:NS, :], a_seq[:, :, :], start=True, stop=True).then_inc(dt_sum, 1)

                def first(c, u, nt):
                    pe.wait_ge(chunk_in[u], 32 * (c // 2) + 32 if isinstance(c, int) else 16 * (c - u) + 32)
                    if known_at_least(c, 1):
                        pe.wait_ge(x_ready, c)
                    for k in range(4):
                        last = pe.transpose(psX[0:nt, k, :], xbc[:, u, k, 0:nt], ident[:, :])
                    last.then_inc(x_turned, 1)
                    if known_at_least(c, 1):
                        pe.wait_ge(b_ready, c)
                    for g in range(2):
                        last = pe.transpose(psB[0:nt, g, :], xbc[:, u, 4 + g, 0:nt], ident[:, :])
                    last.then_inc(b_turned, 1)
                    if known_at_least(c, 1):
                        pe.wait_ge(low_ready, c)
                    for g in range(2):
                        last = pe.matmul(psS[0:nt, g, 0:nt], xbc[:, u, 4 + g, 0:nt], xbc[:, u, 6 + g, 0:nt], start=True, stop=True)
                    last.then_inc(s_done, 1)
                    pe.wait_ge(cur_ready, c + 1)
                    if known_at_least(c, 1):
                        pe.wait_ge(seg_ready, c)
                    low = (upper if nt == P else upper_s)[0:nt, 0:nt]
                    for h in range(HB):
                        last = pe.matmul(psD[h // 4][:, h % 4, 0:nt], cur[0:nt, u, A_, h:h + 1].to_broadcast([nt, P]), low, start=True, stop=True)
                    last.then_inc(d_done, 1)

                def second(c, u, nt):
                    pe.wait_ge(x_ready, c + 1)
                    pe.wait_ge(mix_ready, c + 1)
                    pe.wait_ge(c_ready, c + 1)
                    if nt == P and known_at_least(c, 1):
                        pe.wait_ge(state_ready, c)
                    if nt != P:
                        pe.wait_ge(s_state_in, 16)
                        pe.wait_ge(state_ready, c)
                    if known_at_least(c, 1):
                        pe.wait_ge(skipped, c)
                    for h in range(HB):
                        rows = slice(HD * (h % 2), HD * (h % 2) + HD)
                        pe.matmul(psY[rows, h // 2, 0:nt], xdt[0:nt, u, h * HD:(h + 1) * HD], mix[0:nt, u, h, 0:nt], start=True, stop=False)
                        if nt == P:
                            last = pe.matmul(psY[rows, h // 2, :], state[:, u, h * HD:(h + 1) * HD], c_dec[:, u, h, :], start=False, stop=True)
                        else:
                            for n in range(DEC_N):
                                cols = slice(n * DEC_T, (n + 1) * DEC_T)
                                last = pe.matmul(psY[rows, h // 2, cols], state_s[:, n, h * HD:(h + 1) * HD], c_dec[:, u, h, cols],
                                                 start=False, stop=n == DEC_N - 1)
                    last.then_inc(y_done, 1)
                    pe.wait_ge(b_ready, c + 1)
                    if nt == P:
                        for g in range(2):
                            last = pe.matmul(psH[:, g * 256:(g + 1) * 256], b_tok[:, u, g, :], xte[:, u, g * 256:(g + 1) * 256], start=True, stop=True)
                        last.then_inc(h_done, 1)
                    else:
                        for n in range(DEC_N):
                            pe.wait_ge(picked, n + 1)
                            if n >= 1:
                                pe.wait_ge(s_state_ready, n)
                            for g in range(2):
                                last = pe.matmul(psH[:, g * 256:(g + 1) * 256], b_tok[0:NS, u, g, :], xte_s[:, n % 2, g * 256:(g + 1) * 256], start=True, stop=True)
                            last.then_inc(hs_done, 1)

                def third(c, u, nt):
                    pe.wait_ge(sq_ready, c + 1)
                    if known_at_least(c, 1):
                        pe.wait_ge(rs_ready, c)
                    for g in range(2):
                        for i in range(2):
                            last = pe.matmul(psG[:, g, 0:nt], ones[:, :], ysq[:, u, 2 * g + i, 0:nt], start=i == 0, stop=i == 1)
                    last.then_inc(g_done, 1)
                chunks(pe, first, second, third)
    return a




def lines_at(io, kind, offset, aps):
    t = io["lines"]
    return bass.AP(t.tensor, kind * 4 * P * LINE + offset, aps)


def bias_lines(nc, io, before):
    with ExitStack() as ctx:
        a = Alloc(nc, ctx, "line", before)
        table = a.sb("table", [33, 8])
        hot = a.sb("hot", [33, 3 * LINE])
        line = a.sb("line", [8, 3, LINE])
        ps = [a.ps(f"ps{i}", [8, LINE]) for i in range(3)]
        ready, hot_in, done, taken, out = (a.sem(s) for s in ("ready", "hot_in", "done", "taken", "out"))
        with nc.Block() as block:
            @block.gpsimd
            def _(pool):
                a.clear_last(pool)
                pool.memset(table[:, :], 1.0).then_inc(ready, 1)

            @block.sync
            def _(sp):
                sp.dma_start(hot[:, :], io["hot"]).then_inc(hot_in, 16)
                sp.wait_ge(ready, 1)
                sp.dma_start(table[0:32, :], io["rel_bias"]).then_inc(hot_in, 16)
                sp.wait_ge(taken, 3)
                for kind in range(4):
                    heads = slice(0, 4) if kind == 0 else slice(4, 8)
                    src = line[heads, max(kind - 1, 0), :].unsqueeze(1).to_broadcast([4, P, LINE])
                    sp.dma_start(io["lines"][kind * 4:kind * 4 + 4, :, :], src).then_inc(out, 16)
                sp.wait_ge(out, 64)

            @block.tensor
            def _(pe):
                pe.wait_ge(hot_in, 32)
                for i in range(3):
                    pe.matmul(ps[i][:, :], table[:, :], hot[:, i * LINE:(i + 1) * LINE], start=True, stop=True).then_inc(done, 1)

            @block.vector
            def _(dve):
                for i in range(3):
                    dve.wait_ge(done, i + 1)
                    dve.tensor_copy(line[:, i, :], ps[i][:, :]).then_inc(taken, 1)
    return a


def attend(nc, io, before):
    with ExitStack() as ctx:
        a = Alloc(nc, ctx, "att", before)
        R = 4
        ident = a.sb("ident", [P, P])
        bias = a.sb("bias", [P, 4, 4, 2 * P])
        sink = a.sb("sink", [P, 4])
        ones = a.sb("ones", [P, 256])
        ones_set = a.sem("ones_set")
        qkv = a.sb("qkv", [P, R, 768])
        qk_t = a.sb("qk_t", [P, R, 4, P])
        v_hi = a.sb("v_hi", [P, R, 256], F16)
        v_lo = a.sb("v_lo", [P, R, 256], F16)
        p = a.sb("p", [P, R, 4, 2 * P])
        p_hi = a.sb("p_hi", [P, R, 8, P], F16)
        p_lo = a.sb("p_lo", [P, R, 8, P], F16)
        neg = a.sb("neg", [P, R, 4])
        o = a.sb("o", [P, R, OROW])
        psT = a.ps("psT", [P, 4, P])
        psS = [[a.ps(f"psS{i}{j}", [P, 2, 2 * P]) for j in range(2)] for i in range(2)]
        psP = [a.ps(f"psP{i}", [P, 4, P]) for i in range(2)]
        psO = a.ps("psO", [P, 256])
        const_in, tile_in, o_out = a.sem("const_in"), a.sems("tile_in", R), a.sems("o_out", R)
        turned, qk_ready, vh_ready, v_ready, s_done, top, maxed, neg_ready, p_ready = (
            a.sem(s) for s in ("turned", "qk_ready", "vh_ready", "v_ready", "s_done", "top", "maxed", "neg_ready", "p_ready"))
        p_turned, hi_ready, lo_ready, o_done, o_ready = (a.sem(s) for s in ("p_turned", "hi_ready", "lo_ready", "o_done", "o_ready"))
        N_CONST = 6

        def rows(kind, i, j):
            if kind < 2:
                return (4 * i + j) * P, 1
            return (j * 512 + i, 4) if kind == 2 else (4 * i + j, 16)

        def tiles(eng, load, score, give):
            def body(kind, i, first):
                n0 = 16 * kind + 4 * i
                for s in range(R + 2):
                    for f, j in ((load, s), (score, s - 1), (give, s - 2)):
                        if 0 <= j < R:
                            f(kind, i, n0 + j, j, kind < 3 and not (first and j == 0))
            for kind in range(4):
                if kind < 2:
                    body(kind, 0, True)
                with eng.Fori(1 if kind < 2 else 0, 4) as i:
                    body(kind, i, kind >= 2)

        def past(n, k=R):
            return known_at_least(n, k)

        def place(kind, h):
            if kind == 0:
                return h % 2, 2, HD * (h // 2), HD * (h // 2), h // 2, h % 2
            return h // 2, 2 + h // 2, HD * (h % 2), HD * h, h % 2, h // 2

        def nothing(*_):
            pass

        with nc.Block() as block:
            @block.sync
            def _(sp):
                sp.dma_start(ident[:, :], io["ident"]).then_inc(const_in, 16)
                sp.dma_start(sink[:, :], io["a_sinks"].partition_broadcast(P)).then_inc(const_in, 16)
                for kind in range(4):
                    sp.dma_start(bias[:, kind, :, :], lines_at(io, kind, P - 1, [[LINE - 1, P], [P * LINE, 4], [1, 2 * P]])).then_inc(const_in, 16)

                def load(kind, i, n, j, prev):
                    if past(n):
                        sp.wait_ge(turned, n - R + 1)
                        sp.wait_ge(v_ready, n - R + 1)
                    start, step = rows(kind, i, j)
                    w = 512 if kind == 0 else 768
                    c0 = 0 if kind == 0 else 512
                    sp.dma_start(qkv[:, j, 0:w], io["tok"][bass.ds(start, P, step), c0:c0 + w]).then_inc(tile_in[j], 16)

                def give(kind, i, n, j, prev):
                    sp.wait_ge(o_ready, n + 1)
                    start, step = rows(kind, i, j)
                    sp.dma_start(io["sums"][kind, bass.ds(start, P, step), :], o[:, j, :]).then_inc(o_out[j], 16)
                tiles(sp, load, nothing, give)
                for j in range(R):
                    sp.wait_ge(o_out[j], 16 * 64 // R)

            @block.gpsimd
            def _(pool):
                a.clear_last(pool)
                pool.memset(ones[:, :], 1.0).then_inc(ones_set, 1)
                pool.wait_ge(ones_set, 1)

                def load(kind, i, n, j, prev):
                    pool.wait_ge(tile_in[j], 16 * (n // R) + 16 if isinstance(n, int) else 4 * (n - j) + 16)
                    if past(n, R - 1):
                        pool.wait_ge(o_done, n - R + 2)
                    c0, w = (384, 128) if kind == 0 else (512, 256)
                    pool.tensor_tensor(v_hi[:, j, 0:w], qkv[:, j, c0:c0 + w], ones[:, 0:w], ALU.mult).then_inc(vh_ready, 1)
                    pool.wait_ge(vh_ready, n + 1)
                    pool.tensor_tensor(v_lo[:, j, 0:w], qkv[:, j, c0:c0 + w], v_hi[:, j, 0:w], ALU.subtract).then_inc(v_ready, 1)
                tiles(pool, load, nothing, nothing)

            @block.scalar
            def _(act):
                act.wait_ge(const_in, 16 * N_CONST)

                def load(kind, i, n, j, prev):
                    w = 3 if kind == 0 else 4
                    if past(n, R - 1):
                        act.wait_ge(s_done, n - R + 2)
                    act.wait_ge(turned, n + 1)
                    act.activation(qk_t[:, j, 0:w, :], psT[:, 0:w, :], ACT.Copy).then_inc(qk_ready, 1)

                def score(kind, i, n, j, prev):
                    cols = slice(0, 2 * P) if prev else slice(P, 2 * P)
                    act.wait_ge(neg_ready, n + 1)
                    for h in range(4):
                        last = act.activation(p[:, j, h, cols], p[:, j, h, cols], ACT.Exp, bias=neg[:, j, h:h + 1],
                                              accum_out=o[:, j, 260 + h:261 + h])
                    last.then_inc(p_ready, 1)

                def give(kind, i, n, j, prev):
                    for b in range(2):
                        act.wait_ge(p_turned, 2 * n + b + 1)
                        if past(n) and b == 0:
                            act.wait_ge(o_done, n - R + 1)
                        if prev:
                            src, dst = psP[b][:, :, :], p_hi[:, j, 4 * b:4 * b + 4, :]
                        else:
                            src, dst = psP[b][:, 1::2, :], p_hi[:, j, 4 * b + 1:4 * b + 4:2, :]
                        act.activation(dst, src, ACT.Copy).then_inc(hi_ready, 1)
                tiles(act, load, score, give)

            @block.vector
            def _(dve):
                dve.wait_ge(const_in, 16 * N_CONST)

                def score(kind, i, n, j, prev):
                    cols = slice(0, 2 * P) if prev else slice(P, 2 * P)
                    dve.wait_ge(s_done, n + 1)
                    if past(n):
                        dve.wait_ge(p_turned, 2 * (n - R + 1))
                        dve.wait_ge(o_out[j], 16 * (n // R) if isinstance(n, int) else 4 * (n - j))
                    dve.memset(neg[:, j, :], 0.0)
                    for h in range(4):
                        *_, bank, at = place(kind, h)
                        last = dve.tensor_tensor_reduce(p[:, j, h, cols], psS[j % 2][bank][:, at, cols], bias[:, kind, h, cols],
                                                        1.0, NEG, ALU.add, ALU.max, o[:, j, 256 + h:257 + h])
                    last.then_inc(top, 1)
                    dve.wait_ge(top, n + 1)
                    if kind == 0:
                        dve.tensor_tensor(o[:, j, 256:260], o[:, j, 256:260], sink[:, :], ALU.max).then_inc(maxed, 1)
                        dve.wait_ge(maxed, n + 1)
                    dve.tensor_scalar(neg[:, j, :], o[:, j, 256:260], -1.0, None, ALU.mult).then_inc(neg_ready, 1)

                def give(kind, i, n, j, prev):
                    for b in range(2):
                        dve.wait_ge(hi_ready, 2 * n + b + 1)
                        if past(n) and b == 0:
                            dve.wait_ge(o_done, n - R + 1)
                        if prev:
                            src, dst, hi = psP[b][:, :, :], p_lo[:, j, 4 * b:4 * b + 4, :], p_hi[:, j, 4 * b:4 * b + 4, :]
                        else:
                            src, dst, hi = psP[b][:, 1::2, :], p_lo[:, j, 4 * b + 1:4 * b + 4:2, :], p_hi[:, j, 4 * b + 1:4 * b + 4:2, :]
                        dve.tensor_tensor(dst, src, hi, ALU.subtract).then_inc(lo_ready, 1)
                    dve.wait_ge(o_done, n + 1)
                    dve.tensor_copy(o[:, j, 0:256], psO[:, :]).then_inc(o_ready, 1)
                tiles(dve, nothing, score, give)

            @block.tensor
            def _(pe):
                pe.wait_ge(const_in, 16 * N_CONST)

                def load(kind, i, n, j, prev):
                    pe.wait_ge(tile_in[j], 16 * (n // R) + 16 if isinstance(n, int) else 4 * (n - j) + 16)
                    if past(n, 1):
                        pe.wait_ge(qk_ready, n)
                    if kind == 0:
                        for q in range(2):
                            pe.transpose(psT[:, q, :], qkv[:, j, q * P:(q + 1) * P], ident[:, :])
                        last = pe.transpose(psT[:, 2, :], qkv[:, j, 256:384], ident[:, :])
                    else:
                        for q in range(4):
                            last = pe.transpose(psT[:, q, :], qkv[:, j, q * P:(q + 1) * P], ident[:, :])
                    last.then_inc(turned, 1)

                def score(kind, i, n, j, prev):
                    pe.wait_ge(qk_ready, n + 1)
                    if past(n, 2):
                        pe.wait_ge(top, n - 1)
                    for h in ((0, 2, 1, 3) if kind == 0 else range(4)):
                        qs, ks, at, _, bank, k = place(kind, h)
                        for half in ((0, 1) if prev else (1,)):
                            slot = j if half else (j - 1) % R
                            last = pe.matmul(psS[j % 2][bank][:, k, half * P:(half + 1) * P], qk_t[at:at + HD, j, qs, :],
                                             qk_t[at:at + HD, slot, ks, :], start=True, stop=True)
                    last.then_inc(s_done, 1)

                def give(kind, i, n, j, prev):
                    pe.wait_ge(p_ready, n + 1)
                    for b in range(2):
                        if past(n, 1):
                            pe.wait_ge(lo_ready, 2 * (n - 1) + b + 1)
                        for h in range(2):
                            for half in ((0, 1) if prev else (1,)):
                                last = pe.transpose(psP[b][:, 2 * h + half, :], p[:, j, 2 * b + h, half * P:(half + 1) * P], ident[:, :])
                        last.then_inc(p_turned, 1)
                    pe.wait_ge(v_ready, n + 1)
                    if past(n, 1):
                        pe.wait_ge(o_ready, n)
                    for h in range(4):
                        vc = place(kind, h)[3]
                        if h % 2 == 0:
                            pe.wait_ge(lo_ready, 2 * n + h // 2 + 1)
                        halves = (0, 1) if prev else (1,)
                        for half in halves:
                            slot = j if half else (j - 1) % R
                            cols = slice(vc, vc + HD)
                            for k, (ps, vs) in enumerate(((p_hi, v_hi), (p_hi, v_lo), (p_lo, v_hi))):
                                last = pe.matmul(psO[:, h * HD:(h + 1) * HD], ps[:, j, 2 * h + half, :], vs[:, slot, cols],
                                                 start=half == halves[0] and k == 0, stop=half == 1 and k == 2)
                    last.then_inc(o_done, 1)
                tiles(pe, load, score, give)
    return a



def join(nc, io, before):
    with ExitStack() as ctx:
        a = Alloc(nc, ctx, "join", before)
        ident = a.sb("ident", [P, P])
        sink = a.sb("sink", [P, 4])
        s = a.sb("s", [P, 2, 4, OROW])
        m = a.sb("m", [P, 2, 4])
        e = a.sb("e", [P, 2, 4, 4])
        w = a.sb("w", [P, 2, 4, 4])
        den = a.sb("den", [P, 2, 2, 4])
        f = a.sb("f", [P, 2, 4, 4])
        t = a.sb("t", [P, 2, 4, 256])
        hi = a.sb("hi", [P, 2, 4, P], F16)
        lo = a.sb("lo", [P, 2, 4, P], F16)
        ps = [a.ps(f"ps{i}", [P, 4, P]) for i in range(2)]
        const_in, s_in, out = a.sem("const_in"), a.sems("s_in", 2), a.sems("out", 2)
        step, e_ready, o_ready, turned, hi_ready, lo_ready = (a.sem(x) for x in ("step", "e_ready", "o_ready", "turned", "hi_ready", "lo_ready"))
        STEPS = 12

        def tiles(eng, fs):
            def pair(n):
                for f_ in fs:
                    for u in range(2):
                        f_(n + u, u)
            pair(0)
            with eng.Fori(1, NT // 2) as i:
                pair(2 * i)

        def uses(n, u, inc):
            return inc * (n // 2) if isinstance(n, int) else (inc // 2) * (n - u)

        hi_of = io["mix_hi"].rearrange("(k p) t -> p k t", p=P)
        lo_of = io["mix_lo"].rearrange("(k p) t -> p k t", p=P)
        with nc.Block() as block:
            @block.gpsimd
            def _(pool):
                a.clear_last(pool)

            @block.sync
            def _(sp):
                sp.dma_start(ident[:, :], io["ident"]).then_inc(const_in, 16)
                sp.dma_start(sink[:, :], io["a_sinks"].partition_broadcast(P)).then_inc(const_in, 16)

                def load(n, u):
                    if known_at_least(n, 2):
                        sp.wait_ge(o_ready, n - 1)
                    sp.dma_start(s[:, u, :, :], io["sums"][:, bass.ds(n * P, P), :].rearrange("k p c -> p k c")).then_inc(s_in[u], 16)

                tiles(sp, (load,))

            @block.scalar
            def _(act):
                def exps(n, u):
                    act.wait_ge(step, STEPS * n + 4)
                    act.activation(e[:, u, :, :], e[:, u, :, :], ACT.Exp).then_inc(e_ready, 1)

                def highs(n, u):
                    act.wait_ge(turned, n + 1)
                    if known_at_least(n, 2):
                        act.wait_ge(out[u], uses(n, u, 64))
                    act.activation(hi[:, u, :, :], ps[u][:, :, :], ACT.Copy).then_inc(hi_ready, 1)

                def store(n, u):
                    for tile, of, ready in ((hi, hi_of, hi_ready), (lo, lo_of, lo_ready)):
                        act.wait_ge(ready, n + 1)
                        act.dma_start(of[:, 0:2, bass.ds(n * P, P)], tile[:, u, 0:2, :]).then_inc(out[u], 16)
                        act.dma_start(of[:, 6:8, bass.ds(n * P, P)], tile[:, u, 2:4, :]).then_inc(out[u], 16)
                tiles(act, (exps, highs, store))
                act.wait_ge(out[0], 64 * NT // 2)
                act.wait_ge(out[1], 64 * NT // 2)

            @block.vector
            def _(dve):
                dve.wait_ge(const_in, 32)

                def weigh(n, u):
                    count = [0]

                    def then(ins):
                        count[0] += 1
                        ins.then_inc(step, 1)
                        dve.wait_ge(step, STEPS * n + count[0])

                    dve.wait_ge(s_in[u], uses(n, u, 16) + 16)
                    if known_at_least(n, 2):
                        dve.wait_ge(turned, n - 1)
                    top, low = s[:, u, :, 256:260], s[:, u, :, 260:264]
                    then(dve.tensor_tensor(m[:, u, :], top[:, 1, :], top[:, 2, :], ALU.max))
                    then(dve.tensor_tensor(m[:, u, :], m[:, u, :], top[:, 3, :], ALU.max))
                    then(dve.tensor_tensor(e[:, u, 1:4, :], top[:, 1:4, :], m[:, u, :].unsqueeze(1).to_broadcast([P, 3, 4]), ALU.subtract))
                    then(dve.tensor_tensor(e[:, u, 0, :], sink[:, :], top[:, 0, :], ALU.subtract))
                    dve.wait_ge(e_ready, n + 1)
                    then(dve.tensor_tensor(w[:, u, :, :], e[:, u, :, :], low, ALU.mult))
                    then(dve.tensor_tensor(den[:, u, 0, :], low[:, 0, :], e[:, u, 0, :], ALU.add))
                    then(dve.tensor_tensor(den[:, u, 1, :], w[:, u, 1, :], w[:, u, 2, :], ALU.add))
                    then(dve.tensor_tensor(den[:, u, 1, :], den[:, u, 1, :], w[:, u, 3, :], ALU.add))
                    then(dve.reciprocal(den[:, u, :, :], den[:, u, :, :]))
                    dve.tensor_copy(f[:, u, 0, :], den[:, u, 0, :])
                    then(dve.tensor_tensor(f[:, u, 1:4, :], e[:, u, 1:4, :], den[:, u, 1, :].unsqueeze(1).to_broadcast([P, 3, 4]), ALU.mult))
                    for k in range(4):
                        last = dve.tensor_tensor(t[:, u, k, :].rearrange("p (h d) -> p h d", d=HD), s[:, u, k, 0:256].rearrange("p (h d) -> p h d", d=HD),
                                                 spread(f[:, u, k, :], [P, 4, HD]), ALU.mult)
                    then(last)
                    then(dve.tensor_tensor(t[:, u, 1, :], t[:, u, 1, :], t[:, u, 2, :], ALU.add))
                    dve.tensor_tensor(t[:, u, 1, :], t[:, u, 1, :], t[:, u, 3, :], ALU.add).then_inc(o_ready, 1)
                    assert count[0] == STEPS

                def lows(n, u):
                    dve.wait_ge(hi_ready, n + 1)
                    dve.tensor_tensor(lo[:, u, :, :], ps[u][:, :, :], hi[:, u, :, :], ALU.subtract).then_inc(lo_ready, 1)
                tiles(dve, (weigh, lows))

            @block.tensor
            def _(pe):
                pe.wait_ge(const_in, 32)

                def turn(n, u):
                    pe.wait_ge(o_ready, n + 1)
                    if known_at_least(n, 2):
                        pe.wait_ge(lo_ready, n - 1)
                    for k in range(4):
                        last = pe.transpose(ps[u][:, k, :], t[:, u, k // 2, (k % 2) * P:(k % 2 + 1) * P], ident[:, :])
                    last.then_inc(turned, 1)
                tiles(pe, (turn,))
    return a




def attend_sample(nc, io, before):
    with ExitStack() as ctx:
        a = Alloc(nc, ctx, "smp", before)
        NQ, NH, KC = 8, 14, 9
        ident = a.sb("ident", [P, P])
        masks = a.sb("masks", [P, 2, NS])
        sink = a.sb("sink", [P, 1])
        b_old = a.sb("b_old", [P, 4, P])
        b_new = a.sb("b_new", [P, 4, DEC_T])
        b_all = a.sb("b_all", [P, 4, NS])
        tok = a.sb("tok", [NS, QKV])
        vn_hi = a.sb("vn_hi", [NS, 384], F16)
        vn_lo = a.sb("vn_lo", [NS, 384], F16)
        q_hi = a.sb("q_hi", [HD, NH, NS], F16)
        q_lo = a.sb("q_lo", [HD, NH, NS], F16)
        qn = a.sb("qn", [HD, 2, 2, NQ, DEC_T], F16)
        ka = a.sb("ka", [HD, 2, 2, P])
        kc = a.sb("kc", [HD, 2, 4, KC * P])
        ka_hi = a.sb("ka_hi", [HD, 2, 2, P], F16)
        ka_lo = a.sb("ka_lo", [HD, 2, 2, P], F16)
        kc_hi = a.sb("kc_hi", [HD, 2, 4, KC * P], F16)
        kc_lo = a.sb("kc_lo", [HD, 2, 4, KC * P], F16)
        v = a.sb("v", [P, 2, KC * 256 + P])
        v_hi = a.sb("v_hi", [P, 2, KC * 256 + P], F16)
        v_lo = a.sb("v_lo", [P, 2, KC * 256 + P], F16)
        st = a.sb("st", [P, 16, NS])
        sc = a.sb("sc", [P, 4, P + NS])
        top = a.sb("top", [P, 2])
        den = a.sb("den", [P, 4])
        rden = a.sb("rden", [P, 2])
        es = a.sb("es", [P, 1])
        pn = a.sb("pn", [P, 2, NS])
        pt_hi = a.sb("pt_hi", [P, 16, NS], F16)
        pt_lo = a.sb("pt_lo", [P, 16, NS], F16)
        pn_hi = a.sb("pn_hi", [NS, 8, NS], F16)
        pn_lo = a.sb("pn_lo", [NS, 8, NS], F16)
        pc = a.sb("pc", [P, 2, 2, 16, DEC_T], F16)
        ot = a.sb("ot", [HD, 8, NS])
        o_hi = a.sb("o_hi", [HD, 8, NS], F16)
        o_lo = a.sb("o_lo", [HD, 8, NS], F16)
        psQ, psN, psR = a.ps("psQ", [HD, NH, NS]), a.ps("psN", [P, 2, NS]), a.ps("psR", [P, 4, P])
        psS = [a.ps(f"psS{i}", [P, 16, DEC_T]) for i in range(2)]
        psP, psM = a.ps("psP", [P, 4, P]), a.ps("psM", [NS, 2, P])
        const_in, k_in, v_in, out = a.sem("const_in"), a.sems("k_in", 2), a.sems("v_in", 2), a.sem("out")
        q_turned, q_hi_ready, q_ready, vn_hi_ready, vn_ready = (a.sem(s) for s in ("q_turned", "q_hi_ready", "q_ready", "vn_hi_ready", "vn_ready"))
        k_hi_ready, k_ready, qn_ready, s_done, s_taken, n_done, r_turned = (
            a.sem(s) for s in ("k_hi_ready", "k_ready", "qn_ready", "s_done", "s_taken", "n_done", "r_turned"))
        step, exped, p_turned, pt_hi_ready, pt_ready = (a.sem(s) for s in ("step", "exped", "p_turned", "pt_hi_ready", "pt_ready"))
        v_hi_ready, v_ready, pc_ready, o_done, o_taken, on_done, o_sum, o_hi_ready, o_ready = (
            a.sem(s) for s in ("v_hi_ready", "v_ready", "pc_ready", "o_done", "o_taken", "on_done", "o_sum", "o_hi_ready", "o_ready"))
        slot_of = (0, 2, 1, 3)
        N_CONST = 4 + 32

        def sequences(eng, f):
            f(0, 0)
            f(1, 1)
            with eng.Fori(1, DEC_N // 2) as i:
                for u in range(2):
                    f(2 * i + u, u)

        def past(n):
            return known_at_least(n, 2)

        def arrived(n, u, inc):
            return inc * (n // 2) + inc if isinstance(n, int) else (inc // 2) * (n - u) + inc

        with nc.Block() as block:
            @block.sync
            def _(sp):
                sp.dma_start(ident[:, :], io["ident"]).then_inc(const_in, 16)
                sp.dma_start(masks[:, :, :], io["masks_s"]).then_inc(const_in, 16)
                sp.dma_start(tok[:, :], io["tok"][SEQ:TOK, 0:QKV]).then_inc(const_in, 16)
                s = io["a_sinks"]
                sp.dma_start(sink[:, :], bass.AP(s.tensor, 0, [[1, 4], [0, NS], [1, 1]]), allow_slow_non_contiguous=True).then_inc(const_in, 16)

                def load_k(n, u):
                    if past(n):
                        sp.wait_ge(k_hi_ready, n - 1)
                        sp.wait_ge(k_ready, n - 1)
                    sp.dma_start(kc[:, u, :, :], io["c_kt"][bass.ds(n, 1), :, :, :].rearrange("n d h k -> (n d) h k")).then_inc(k_in[u], 16)
                    sp.dma_start(ka[:, u, :, :], io["a_kt"][bass.ds(n, 1), :, :, :].rearrange("n d h k -> (n d) h k")).then_inc(k_in[u], 16)
                load_k(0, 0)
                load_k(1, 1)
                for kind in range(4):
                    for h in range(4):
                        rows = slice(NS * h, NS * h + NS)
                        near = h * P * LINE
                        t_step = LINE - 1 if kind < 2 else 0
                        sp.dma_start(b_old[rows, kind, :], lines_at(io, kind, near + P - 1, [[0, DEC_N], [t_step, DEC_T], [1, P]])).then_inc(const_in, 16)
                        sp.dma_start(b_new[rows, kind, :], lines_at(io, kind, near + 2 * P - 1, [[0, DEC_N], [LINE - 1, DEC_T], [1, DEC_T]])).then_inc(const_in, 16)
                with sp.Fori(1, DEC_N // 2) as i:
                    for u in range(2):
                        load_k(2 * i + u, u)

                def load_v(n, u):
                    if past(n):
                        sp.wait_ge(v_ready, n - 1)
                    sp.dma_start(v[:, u, 0:KC * 256], io["c_v"][bass.ds(n, 1), :, :].rearrange("n k c -> (n k) c")).then_inc(v_in[u], 16)
                    sp.dma_start(v[:, u, KC * 256:], io["a_v"][bass.ds(n, 1), :, :].rearrange("n k c -> (n k) c")).then_inc(v_in[u], 16)
                sequences(sp, load_v)
                for tile, dst, ready in ((o_hi, io["mix_hi"], o_hi_ready), (o_lo, io["mix_lo"], o_ready)):
                    sp.wait_ge(ready, 1)
                    sp.dma_start(dst[0:256, SEQ:TOK].rearrange("(h d) t -> d h t", d=HD), tile[:, 0:4, :]).then_inc(out, 16)
                    sp.dma_start(dst[768:1024, SEQ:TOK].rearrange("(h d) t -> d h t", d=HD), tile[:, 4:8, :]).then_inc(out, 16)
                sp.wait_ge(out, 64)

            @block.scalar
            def _(act):
                act.wait_ge(const_in, 16 * N_CONST)
                act.wait_ge(q_turned, 1)
                act.activation(q_hi[:, :, :], psQ[:, :, :], ACT.Copy).then_inc(q_hi_ready, 1)

                def split_k(n, u):
                    act.wait_ge(k_in[u], arrived(n, u, 32))
                    if past(n):
                        act.wait_ge(s_done, n - 1)
                    act.activation(ka_hi[:, u, :, :], ka[:, u, :, :], ACT.Copy)
                    act.activation(kc_hi[:, u, :, :], kc[:, u, :, :], ACT.Copy).then_inc(k_hi_ready, 1)
                sequences(act, split_k)
                act.wait_ge(step, 4)
                act.activation(es[:, :], sink[:, :], ACT.Exp, bias=top[:, 0:1]).then_inc(exped, 1)
                for kind in range(4):
                    act.activation(sc[:, kind, :], sc[:, kind, :], ACT.Exp, bias=top[:, min(kind, 1):min(kind, 1) + 1],
                                   accum_out=den[:, kind:kind + 1]).then_inc(exped, 1)
                act.wait_ge(p_turned, 1)
                act.activation(pt_hi[:, :, :], psP[:, :, :].rearrange("p k (h t) -> p (k h) t", t=NS), ACT.Copy)
                act.activation(pn_hi[:, :, :], psM[:, :, :].rearrange("p k (h t) -> p (k h) t", t=NS), ACT.Copy).then_inc(pt_hi_ready, 1)

                def split_v(n, u):
                    act.wait_ge(v_in[u], arrived(n, u, 32))
                    if past(n):
                        act.wait_ge(o_done, n - 1)
                    act.activation(v_hi[:, u, :], v[:, u, :], ACT.Copy).then_inc(v_hi_ready, 1)
                sequences(act, split_v)
                act.wait_ge(o_sum, 1)
                act.activation(o_hi[:, :, :], ot[:, :, :], ACT.Copy).then_inc(o_hi_ready, 1)

            @block.gpsimd
            def _(pool):
                a.clear_last(pool)
                pool.wait_ge(const_in, 16 * N_CONST)
                pool.tensor_copy(vn_hi[:, 0:P], tok[:, 384:512])
                pool.tensor_copy(vn_hi[:, P:384], tok[:, 1024:1280]).then_inc(vn_hi_ready, 1)
                pool.wait_ge(vn_hi_ready, 1)
                pool.tensor_tensor(vn_lo[:, 0:P], tok[:, 384:512], vn_hi[:, 0:P], ALU.subtract)
                pool.tensor_tensor(vn_lo[:, P:384], tok[:, 1024:1280], vn_hi[:, P:384], ALU.subtract).then_inc(vn_ready, 1)

            @block.vector
            def _(dve):
                dve.wait_ge(const_in, 16 * N_CONST)
                dve.wait_ge(q_hi_ready, 1)
                for kind in range(4):
                    dve.tensor_tensor(b_all[:, kind, :].rearrange("p (n t) -> p n t", t=DEC_T), b_new[:, kind, :].unsqueeze(1).to_broadcast([P, DEC_N, DEC_T]),
                                      masks[:, kind // 2, :].rearrange("p (n t) -> p n t", t=DEC_T), ALU.add)
                dve.tensor_tensor(q_lo[:, :, :], psQ[:, :, :], q_hi[:, :, :], ALU.subtract).then_inc(q_ready, 1)
                dve.wait_ge(q_ready, 1)

                def split_k(n, u):
                    if past(n):
                        dve.wait_ge(s_done, n - 1)
                    for i, q in enumerate((q_hi, q_lo)):
                        last = dve.tensor_copy(qn[:, u, i, :, :], q[:, 0:NQ, bass.ds(n * DEC_T, DEC_T)])
                    last.then_inc(qn_ready, 1)
                    dve.wait_ge(k_hi_ready, n + 1)
                    dve.tensor_tensor(ka_lo[:, u, :, :], ka[:, u, :, :], ka_hi[:, u, :, :], ALU.subtract)
                    dve.tensor_tensor(kc_lo[:, u, :, :], kc[:, u, :, :], kc_hi[:, u, :, :], ALU.subtract).then_inc(k_ready, 1)
                    dve.wait_ge(s_done, n + 1)
                    dve.tensor_copy(st[:, :, bass.ds(n * DEC_T, DEC_T)], psS[u][:, :, :]).then_inc(s_taken, 1)
                sequences(dve, split_k)

                count = [0]

                def then(ins):
                    count[0] += 1
                    ins.then_inc(step, 1)
                    dve.wait_ge(step, count[0])
                dve.wait_ge(r_turned, 1)
                dve.wait_ge(n_done, 1)
                for kind in range(4):
                    dve.tensor_tensor(sc[:, kind, P:], psN[:, min(kind, 1), :], b_all[:, kind, :], ALU.add)
                then(dve.tensor_tensor(sc[:, :, 0:P], psR[:, :, :], b_old[:, :, :], ALU.add))
                dve.tensor_reduce(top[:, 1:2], sc[:, 1:4, :], AX.XY, ALU.max)
                then(dve.tensor_reduce(top[:, 0:1], sc[:, 0, :], AX.X, ALU.max))
                then(dve.tensor_tensor(top[:, 0:1], top[:, 0:1], sink[:, :], ALU.max))
                then(dve.tensor_scalar(top[:, :], top[:, :], -1.0, None, ALU.mult))
                dve.wait_ge(exped, 5)
                dve.tensor_tensor(rden[:, 0:1], den[:, 0:1], es[:, :], ALU.add)
                then(dve.tensor_reduce(rden[:, 1:2], den[:, 1:4], AX.X, ALU.add))
                then(dve.reciprocal(rden[:, :], rden[:, :]))
                dve.tensor_scalar(sc[:, 0, :], sc[:, 0, :], rden[:, 0:1], None, ALU.mult)
                then(dve.tensor_scalar(sc[:, 1:4, :], sc[:, 1:4, :], rden[:, 1:2], None, ALU.mult))
                dve.tensor_copy(pn[:, 0, :], sc[:, 0, P:])
                then(dve.tensor_tensor(pn[:, 1, :], sc[:, 1, P:], sc[:, 2, P:], ALU.add))
                then(dve.tensor_tensor(pn[:, 1, :], pn[:, 1, :], sc[:, 3, P:], ALU.add))
                dve.wait_ge(pt_hi_ready, 1)
                dve.tensor_tensor(pt_lo[:, :, :], psP[:, :, :].rearrange("p k (h t) -> p (k h) t", t=NS), pt_hi[:, :, :], ALU.subtract)
                dve.tensor_tensor(pn_lo[:, :, :], psM[:, :, :].rearrange("p k (h t) -> p (k h) t", t=NS), pn_hi[:, :, :], ALU.subtract).then_inc(pt_ready, 1)
                dve.wait_ge(pt_ready, 1)

                def split_v(n, u):
                    if past(n):
                        dve.wait_ge(o_done, n - 1)
                    for i, q in enumerate((pt_hi, pt_lo)):
                        last = dve.tensor_copy(pc[:, u, i, :, :], q[:, :, bass.ds(n * DEC_T, DEC_T)])
                    last.then_inc(pc_ready, 1)
                    dve.wait_ge(v_hi_ready, n + 1)
                    dve.tensor_tensor(v_lo[:, u, :], v[:, u, :], v_hi[:, u, :], ALU.subtract).then_inc(v_ready, 1)
                    dve.wait_ge(o_done, n + 1)
                    dve.tensor_copy(ot[:, :, bass.ds(n * DEC_T, DEC_T)], psS[u][0:HD, 0:8, :]).then_inc(o_taken, 1)
                sequences(dve, split_v)
                dve.wait_ge(on_done, 1)
                dve.wait_ge(o_taken, DEC_N)
                dve.tensor_tensor(ot[:, :, :], ot[:, :, :], psQ[:, 0:8, :], ALU.add).then_inc(o_sum, 1)
                dve.wait_ge(o_hi_ready, 1)
                dve.tensor_tensor(o_lo[:, :, :], ot[:, :, :], o_hi[:, :, :], ALU.subtract).then_inc(o_ready, 1)

            @block.tensor
            def _(pe):
                pe.wait_ge(const_in, 16 * N_CONST)
                cols = [64 * i for i in range(4)] + [512 + 64 * i for i in range(4)] + [256, 320] + [768 + 64 * i for i in range(4)]
                for i, c in enumerate(cols):
                    last = pe.transpose(psQ[:, i, :], tok[:, c:c + HD], ident[0:NS, 0:NS])
                last.then_inc(q_turned, 1)
                pe.wait_ge(q_ready, 1)

                def thrice(out, l_hi, l_lo, r_hi, r_lo, start, stop):
                    for i, (l, r) in enumerate(((l_hi, r_hi), (l_hi, r_lo), (l_lo, r_hi))):
                        last = pe.matmul(out, l, r, start=start and i == 0, stop=stop and i == 2)
                    return last

                for h in range(4):
                    for m in range(2):
                        qs = slot_of[h] if m == 0 else 4 + h
                        ks = 8 + h // 2 if m == 0 else 10 + h
                        last = thrice(psN[NS * h:NS * h + NS, m, :], q_hi[:, qs, :], q_lo[:, qs, :], q_hi[:, ks, :], q_lo[:, ks, :], True, True)
                last.then_inc(n_done, 1)

                def score(n, u):
                    pe.wait_ge(k_ready, n + 1)
                    pe.wait_ge(qn_ready, n + 1)
                    if past(n):
                        pe.wait_ge(s_taken, n - 1)
                    for h in range(4):
                        qs = slot_of[h]
                        last = thrice(psS[u][:, h, :], ka_hi[:, u, h // 2, :], ka_lo[:, u, h // 2, :],
                                      qn[:, u, 0, qs, :], qn[:, u, 1, qs, :], True, True)
                        for k in range(KC):
                            t = slice(0, DEC_T) if k == 0 else slice((k - 1) % 4, (k - 1) % 4 + 1)
                            kind = 1 if k == 0 else 2 + (k - 1) // 4
                            keys = slice(k * P, (k + 1) * P)
                            last = thrice(psS[u][:, 4 * kind + h, t], kc_hi[:, u, h, keys], kc_lo[:, u, h, keys],
                                          qn[:, u, 0, 4 + h, t], qn[:, u, 1, 4 + h, t], True, True)
                    last.then_inc(s_done, 1)
                sequences(pe, score)
                pe.wait_ge(s_taken, DEC_N)
                for kind in range(4):
                    last = pe.transpose(psR[:, kind, :], st[:, 4 * kind:4 * kind + 4, :].rearrange("p h t -> p (h t)"), ident[:, :])
                last.then_inc(r_turned, 1)
                pe.wait_ge(step, 9)
                for kind in range(4):
                    pe.transpose(psP[:, kind, :], sc[:, kind, 0:P], ident[:, :])
                for m in range(2):
                    last = pe.transpose(psM[:, m, :], pn[:, m, :], ident[:, :])
                last.then_inc(p_turned, 1)
                pe.wait_ge(pt_ready, 1)
                pe.wait_ge(vn_ready, 1)
                for m in range(2):
                    for h in range(4):
                        c = slice(HD * (h // 2), HD * (h // 2) + HD) if m == 0 else slice(P + HD * h, P + HD * h + HD)
                        s = 4 * m + h
                        last = thrice(psQ[:, s, :], vn_hi[:, c], vn_lo[:, c], pn_hi[:, s, :], pn_lo[:, s, :], True, True)
                last.then_inc(on_done, 1)

                def give(n, u):
                    pe.wait_ge(v_ready, n + 1)
                    pe.wait_ge(pc_ready, n + 1)
                    if past(n):
                        pe.wait_ge(o_taken, n - 1)
                    for h in range(4):
                        c = slice(KC * 256 + HD * (h // 2), KC * 256 + HD * (h // 2) + HD)
                        last = thrice(psS[u][0:HD, h, :], v_hi[:, u, c], v_lo[:, u, c], pc[:, u, 0, h, :], pc[:, u, 1, h, :], True, True)
                    for h in range(4):
                        for k in range(KC):
                            t = slice(0, DEC_T) if k == 0 else slice((k - 1) % 4, (k - 1) % 4 + 1)
                            s = 4 * (1 if k == 0 else 2 + (k - 1) // 4) + h
                            c = slice(k * 256 + HD * h, k * 256 + HD * h + HD)
                            last = thrice(psS[u][0:HD, 4 + h, t], v_hi[:, u, c], v_lo[:, u, c], pc[:, u, 0, s, t], pc[:, u, 1, s, t], k == 0, k == KC - 1)
                    last.then_inc(o_done, 1)
                sequences(pe, give)
    return a




TB = 416
NB = TOK // TB
TR = 104


def out_project(nc, io, h, u_hi, u_lo, before):
    with ExitStack() as ctx:
        a = Alloc(nc, ctx, "out", before)
        w_raw = a.sb("w_raw", [P, D])
        w_hi = a.sb("w_hi", [P, KT, D], F16)
        w_lo = a.sb("w_lo", [P, KT, D], F16)
        x = a.sb("x", [TR, TB // TR, D])
        mix = a.sb("mix", [P, 2, KT, TB], F16)
        sq = a.sb("sq", [P, 2, TB])
        rs = a.sb("rs", [P, TB])
        un = a.sb("un", [P, 2, TB])
        ident = a.sb("ident", [TR, TR])
        ones = a.sb("ones", [P, P])
        g = a.sb("g", [P, KT])
        eps = a.sb("eps", [P, 1])
        psO = [a.ps(f"psO{i}", [P, TB]) for i in range(2)]
        psG = [a.ps(f"psG{i}", [P, TB]) for i in range(2)]
        const_in, made, w_in, x_in, mix_in = (a.sem(s) for s in ("const_in", "made", "w_in", "x_in", "mix_in"))
        w_hi_done, w_lo_done = a.sem("w_hi_done"), a.sem("w_lo_done")
        o_done, o_taken, sq_ready, g_done, g_log, rs_ready, un_ready, hi_ready, lo_ready = (
            a.sem(s) for s in ("o_done", "o_taken", "sq_ready", "g_done", "g_log", "rs_ready", "un_ready", "hi_ready", "lo_ready"))
        N_CONST = 2
        srcs = [io[s].rearrange("(k p) t -> p k t", p=P) for s in ("mix_hi", "mix_lo")]

        def blocks(eng, body):
            body(0)
            with eng.Fori(1, NB) as n:
                body(n)

        with nc.Block() as block:
            @block.sync
            def _(sp):
                sp.dma_start(ident[:, :], io["ident"][0:TR, 0:TR]).then_inc(const_in, 16)
                sp.dma_start(g[:, :], io["norm_mlp_g"]).then_inc(const_in, 16)

                def load(n):
                    if known_at_least(n, 1):
                        sp.wait_ge(o_done, KT * n)
                    sp.dma_start(x[:, :, :], io["x"][bass.ds(n * TB, TB), :].rearrange("(i p) d -> p i d", p=TR)).then_inc(x_in, 16)
                    for i in range(2):
                        sp.dma_start(mix[:, i, :, :], srcs[i][:, :, bass.ds(n * TB, TB)]).then_inc(mix_in, 16)
                load(0)
                for k in range(KT):
                    if k:
                        sp.wait_ge(w_hi_done, k)
                        sp.wait_ge(w_lo_done, k)
                    sp.dma_start(w_raw[:, :], io["w_out"][k * P:(k + 1) * P, :]).then_inc(w_in, 16)
                with sp.Fori(1, NB) as n:
                    load(n)

            @block.gpsimd
            def _(pool):
                a.clear_last(pool)
                pool.memset(ones[:, :], 1.0).then_inc(made, 1)
                pool.memset(eps[:, :], EPS).then_inc(made, 1)
                pool.wait_ge(const_in, 16 * N_CONST)
                pool.tensor_scalar(ident[:, :], ident[:, :], WS, None, ALU.mult).then_inc(made, 1)

            @block.scalar
            def _(act):
                act.wait_ge(const_in, 16 * N_CONST)
                act.wait_ge(made, 3)
                for k in range(KT):
                    act.wait_ge(w_in, 16 * (k + 1))
                    act.activation(w_hi[:, k, :], w_raw[:, :], ACT.Copy, scale=WS).then_inc(w_hi_done, 1)

                def body(n):
                    for m in range(KT):
                        act.wait_ge(o_done, KT * n + m + 1)
                        act.activation(h[:, m, bass.ds(n * TB, TB)], psO[m % 2][:, :], ACT.Copy, scale=1.0 / WS)
                        if known_at_least(n, 1) or m >= 2:
                            act.wait_ge(g_done, KT * n + m - 1)
                        act.activation(sq[:, m % 2, :], psO[m % 2][:, :], ACT.Square, scale=1.0 / WS).then_inc(sq_ready, 1)
                    act.wait_ge(g_done, KT * n + KT)
                    if known_at_least(n, 1):
                        act.wait_ge(un_ready, KT * n)
                    act.activation(rs[:, :], psG[0][:, :], ACT.Ln, bias=eps[:, :], scale=1.0 / D).then_inc(g_log, 1)
                    act.wait_ge(g_log, n + 1)
                    act.activation(rs[:, :], rs[:, :], ACT.Exp, scale=-0.5).then_inc(rs_ready, 1)
                    for m in range(KT):
                        act.wait_ge(un_ready, KT * n + m + 1)
                        act.activation(u_hi[:, m, bass.ds(n * TB, TB)], un[:, m % 2, :], ACT.Copy).then_inc(hi_ready, 1)
                blocks(act, body)

            @block.vector
            def _(dve):
                dve.wait_ge(const_in, 16 * N_CONST)
                for k in range(KT):
                    dve.wait_ge(w_hi_done, k + 1)
                    dve.scalar_tensor_tensor(w_lo[:, k, :], w_raw[:, :], WS, w_hi[:, k, :], ALU.mult, ALU.subtract).then_inc(w_lo_done, 1)

                def body(n):
                    dve.wait_ge(rs_ready, n + 1)

                    def low(m):
                        dve.wait_ge(hi_ready, KT * n + m + 1)
                        dve.tensor_tensor(u_lo[:, m, bass.ds(n * TB, TB)], un[:, m % 2, :], u_hi[:, m, bass.ds(n * TB, TB)], ALU.subtract).then_inc(lo_ready, 1)
                    for m in range(KT):
                        if m >= 2 or known_at_least(n, 1):
                            dve.wait_ge(lo_ready, KT * n + m - 1)
                        dve.scalar_tensor_tensor(un[:, m % 2, :], h[:, m, bass.ds(n * TB, TB)], g[:, m:m + 1], rs[:, :], ALU.mult, ALU.mult).then_inc(un_ready, 1)
                        if m:
                            low(m - 1)
                    low(KT - 1)
                blocks(dve, body)

            @block.tensor
            def _(pe):
                pe.wait_ge(made, 3)

                def square_sum(n, m):
                    pe.wait_ge(sq_ready, KT * n + m + 1)
                    if m == 0 and known_at_least(n, 1):
                        pe.wait_ge(rs_ready, n)
                    pe.matmul(psG[0][:, :], ones[:, :], sq[:, m % 2, :], start=m == 0, stop=m == KT - 1).then_inc(g_done, 1)

                def body(n):
                    pe.wait_ge(x_in, 16 * n + 16)
                    pe.wait_ge(mix_in, 32 * n + 32)
                    for m in range(KT):
                        if known_at_least(n, 1) or m >= 2:
                            pe.wait_ge(sq_ready, KT * n + m - 1)
                        cols = slice(m * P, (m + 1) * P)
                        for i in range(TB // TR):
                            pe.matmul(psO[m % 2][:, i * TR:(i + 1) * TR], x[:, i, cols], ident[:, :], start=i == 0, stop=False, skip_group_check=True)
                        for k in range(KT):
                            if m == 0 and not known_at_least(n, 1):
                                pe.wait_ge(w_lo_done, k + 1)
                            for i, (w, s) in enumerate(((w_hi, 0), (w_hi, 1), (w_lo, 0))):
                                last = pe.matmul(psO[m % 2][:, :], w[:, k, cols], mix[:, s, k, :], start=False,
                                                 stop=k == KT - 1 and i == 2, skip_group_check=True)
                        last.then_inc(o_done, 1)
                        if m:
                            square_sum(n, m - 1)
                    square_sum(n, KT - 1)
                blocks(pe, body)
    return a


def mlp(nc, io, h, u_hi, u_lo, before):
    with ExitStack() as ctx:
        a = Alloc(nc, ctx, "mlp", before)
        FC = 2
        CH = FF // (FC * P)
        up_raw = a.sb("up_raw", [P, KT, FC * P])
        dn_raw = a.sb("dn_raw", [P, FC, D])
        up_hi = a.sb("up_hi", [P, 2, KT, FC * P], F16)
        up_lo = a.sb("up_lo", [P, 2, KT, FC * P], F16)
        dn_hi = a.sb("dn_hi", [P, 2, FC, D], F16)
        dn_lo = a.sb("dn_lo", [P, 2, FC, D], F16)
        r = a.sb("r", [P, FC, TB])
        r2 = a.sb("r2", [P, FC, TB])
        r_hi = a.sb("r_hi", [P, 2, FC, TB], F16)
        r_lo = a.sb("r_lo", [P, 2, FC, TB], F16)
        psU = [[a.ps(f"psU{i}{j}", [P, TB]) for j in range(FC)] for i in range(2)]
        psD = [a.ps(f"psD{i}", [P, TB]) for i in range(4)]
        up_in, dn_in, hi_done, lo_done = (a.sem(s) for s in ("up_in", "dn_in", "hi_done", "lo_done"))
        u_done, r_ready, r2_ready, rh_ready, rl_ready, d_done, d_added = (
            a.sem(s) for s in ("u_done", "r_ready", "r2_ready", "rh_ready", "rl_ready", "d_done", "d_added"))

        def chunks(eng, body):
            for c in range(2):
                body(c, c)
            with eng.Fori(1, CH // 2) as i:
                for s in range(2):
                    body(2 * i + s, s)

        def steps(c, slot, up, down):
            for b in range(NB + 1):
                if b < NB:
                    up(NB * c + b, b, (slot * NB + b) % 2)
                if b >= 1:
                    down(NB * c + b - 1, b - 1, (slot * NB + b - 1) % 2)

        with nc.Block() as block:
            @block.gpsimd
            def _(pool):
                a.clear_last(pool)

            @block.sync
            def _(sp):
                def load(c):
                    if known_at_least(c, 1):
                        sp.wait_ge(lo_done, 2 * c - 1)
                        sp.wait_ge(hi_done, 2 * c - 1)
                    sp.dma_start(up_raw[:, :, :], io["w_up"][:, bass.ds(c * FC * P, FC * P)].rearrange("(k p) f -> p k f", p=P)).then_inc(up_in, 16)
                    if known_at_least(c, 1):
                        sp.wait_ge(lo_done, 2 * c)
                        sp.wait_ge(hi_done, 2 * c)
                    sp.dma_start(dn_raw[:, :, :], io["w_down"][bass.ds(c * FC * P, FC * P), :].rearrange("(f p) d -> p f d", p=P)).then_inc(dn_in, 16)
                load(0)
                with sp.Fori(1, CH) as c:
                    load(c)

            @block.scalar
            def _(act):
                def split(c, slot):
                    if known_at_least(c, 2):
                        act.wait_ge(d_done, KT * NB * (c - 1))
                    act.wait_ge(up_in, 16 * c + 16)
                    act.activation(up_hi[:, slot, :, :], up_raw[:, :, :], ACT.Copy, scale=WS).then_inc(hi_done, 1)
                    act.wait_ge(dn_in, 16 * c + 16)
                    act.activation(dn_hi[:, slot, :, :], dn_raw[:, :, :], ACT.Copy, scale=WS).then_inc(hi_done, 1)

                def up(n, b, s):
                    for f in range(FC):
                        act.wait_ge(u_done, FC * n + f + 1)
                        if known_at_least(n, 1):
                            act.wait_ge(r2_ready, FC * (n - 1) + f + 1)
                        act.activation(r[:, f, :], psU[s][f][:, :], ACT.Relu, scale=1.0 / (WS * HS)).then_inc(r_ready, 1)
                    for f in range(FC):
                        act.wait_ge(r2_ready, FC * n + f + 1)
                        if known_at_least(n, 2):
                            act.wait_ge(d_done, KT * (n - 1))
                        act.activation(r_hi[:, s, f, :], r2[:, f, :], ACT.Copy).then_inc(rh_ready, 1)

                def body(c, slot):
                    for b in range(NB):
                        up(NB * c + b, b, (slot * NB + b) % 2)
                        if b == 2:
                            split(c + 1, 1 - slot)
                split(0, 0)
                for c in range(2):
                    body(c, c)
                with act.Fori(1, CH // 2 - 1) as i:
                    for s in range(2):
                        body(2 * i + s, s)
                body(CH - 2, 0)
                for b in range(NB):
                    up(NB * (CH - 1) + b, b, (NB + b) % 2)

            @block.vector
            def _(dve):
                def split(c, slot):
                    dve.wait_ge(hi_done, 2 * c + 1)
                    dve.scalar_tensor_tensor(up_lo[:, slot, :, :].rearrange("p k f -> p (k f)"), up_raw[:, :, :].rearrange("p k f -> p (k f)"), WS,
                                             up_hi[:, slot, :, :].rearrange("p k f -> p (k f)"), ALU.mult, ALU.subtract).then_inc(lo_done, 1)
                    dve.wait_ge(hi_done, 2 * c + 2)
                    dve.scalar_tensor_tensor(dn_lo[:, slot, :, :].rearrange("p k f -> p (k f)"), dn_raw[:, :, :].rearrange("p k f -> p (k f)"), WS,
                                             dn_hi[:, slot, :, :].rearrange("p k f -> p (k f)"), ALU.mult, ALU.subtract).then_inc(lo_done, 1)

                def up(n, b, s):
                    for f in range(FC):
                        dve.wait_ge(r_ready, FC * n + f + 1)
                        if known_at_least(n, 1):
                            dve.wait_ge(rl_ready, FC * (n - 1) + f + 1)
                        dve.tensor_tensor(r2[:, f, :], r[:, f, :], r[:, f, :], ALU.mult).then_inc(r2_ready, 1)
                    for f in range(FC):
                        dve.wait_ge(rh_ready, FC * n + f + 1)
                        dve.tensor_tensor(r_lo[:, s, f, :], r2[:, f, :], r_hi[:, s, f, :], ALU.subtract).then_inc(rl_ready, 1)

                def down(n, b, s):
                    for m in range(KT):
                        dve.wait_ge(d_done, KT * n + m + 1)
                        if m == 0 and known_at_least(n, NB):
                            dve.wait_ge(d_added, KT * (n - NB + 1))
                        dve.scalar_tensor_tensor(h[:, m, b * TB:(b + 1) * TB], psD[m % 4][:, :], HS * HS / WS, h[:, m, b * TB:(b + 1) * TB],
                                                 ALU.mult, ALU.add).then_inc(d_added, 1)

                def body(c, slot, ahead):
                    def up_and_split(n, b, s):
                        up(n, b, s)
                        if b == 2 and ahead:
                            split(c + 1, 1 - slot)
                    steps(c, slot, up_and_split, down)
                split(0, 0)
                for c in range(2):
                    body(c, c, True)
                with dve.Fori(1, CH // 2 - 1) as i:
                    for s in range(2):
                        body(2 * i + s, s, True)
                body(CH - 2, 0, True)
                body(CH - 1, 1, False)

            @block.tensor
            def _(pe):
                def body(c, slot):
                    def up(n, b, s):
                        if b == 0:
                            pe.wait_ge(lo_done, 2 * c + 1)
                        for f in range(FC):
                            if known_at_least(n, 2):
                                pe.wait_ge(r_ready, FC * (n - 2) + f + 1)
                            cols = slice(f * P, (f + 1) * P)
                            for k in range(KT):
                                for i, (w, u) in enumerate(((up_hi, u_hi), (up_hi, u_lo), (up_lo, u_hi))):
                                    last = pe.matmul(psU[s][f][:, :], w[:, slot, k, cols], u[:, k, b * TB:(b + 1) * TB],
                                                     start=k == 0 and i == 0, stop=k == KT - 1 and i == 2)
                            last.then_inc(u_done, 1)

                    def down(n, b, s):
                        if b == 0:
                            pe.wait_ge(lo_done, 2 * c + 2)
                        pe.wait_ge(rl_ready, FC * n + FC)
                        for m in range(KT):
                            if known_at_least(n, 1) or m >= 4:
                                pe.wait_ge(d_added, KT * n + m - 3)
                            cols = slice(m * P, (m + 1) * P)
                            for f in range(FC):
                                for i, (w, x) in enumerate(((dn_hi, r_hi), (dn_hi, r_lo), (dn_lo, r_hi))):
                                    last = pe.matmul(psD[m % 4][:, :], w[:, slot, f, cols], x[:, s, f, :], start=f == 0 and i == 0, stop=f == FC - 1 and i == 2)
                            last.then_inc(d_done, 1)
                    steps(c, slot, up, down)
                chunks(pe, body)
    return a


def give_back(nc, io, h, before):
    with ExitStack() as ctx:
        a = Alloc(nc, ctx, "y", before)
        S = 3
        ident = a.sb("ident", [P, P])
        y = a.sb("y", [TR, S, D])
        ps = [[a.ps(f"ps{i}{j}", [TR, 4, P]) for j in range(2)] for i in range(S)]
        const_in, turned, halves, y_out = a.sem("const_in"), a.sem("turned"), a.sems("half", 2), a.sems("y_out", S)
        N = TOK // TR
        with nc.Block() as block:
            @block.gpsimd
            def _(pool):
                a.clear_last(pool)

            @block.sync
            def _(sp):
                sp.dma_start(ident[:, :], io["ident"]).then_inc(const_in, 16)
                for n in range(N):
                    for half in halves:
                        sp.wait_ge(half, n + 1)
                    sp.dma_start(io["y"][n * TR:(n + 1) * TR, :], y[:, n % S, :]).then_inc(y_out[n % S], 16)
                for s in range(S):
                    sp.wait_ge(y_out[s], 16 * len(range(s, N, S)))

            @block.tensor
            def _(pe):
                pe.wait_ge(const_in, 16)
                for n in range(N):
                    for half in range(2):
                        if n >= S:
                            pe.wait_ge(halves[half], n - S + 1)
                        for k in range(4):
                            last = pe.transpose(ps[n % S][half][:, k, :], h[:, 4 * half + k, n * TR:(n + 1) * TR], ident[:, :])
                        last.then_inc(turned, 1)

            def take(eng, half):
                for n in range(N):
                    eng.wait_ge(turned, 2 * n + half + 1)
                    if n >= S:
                        eng.wait_ge(y_out[n % S], 16 * (n // S))
                    out, src = y[:, n % S, half * 512:(half + 1) * 512], ps[n % S][half][:, :, :].rearrange("p k d -> p (k d)")
                    if half:
                        nc.scalar.activation(out, src, ACT.Copy).then_inc(halves[1], 1)
                    else:
                        nc.vector.tensor_copy(out, src).then_inc(halves[0], 1)

            @block.scalar
            def _(act):
                take(act, 1)

            @block.vector
            def _(dve):
                take(dve, 0)
    return a




def build(nc, io):
    last = None
    for stage in (project, scan, bias_lines, attend, join, attend_sample):
        last = stage(nc, io, last)
    with ExitStack() as ctx:
        h = ctx.enter_context(nc.sbuf_tensor("h", [P, KT, TOK], F32))
        with ExitStack() as inner:
            u_hi = inner.enter_context(nc.sbuf_tensor("u_hi", [P, KT, TOK], F16))
            u_lo = inner.enter_context(nc.sbuf_tensor("u_lo", [P, KT, TOK], F16))
            last = out_project(nc, io, h, u_hi, u_lo, last)
            last = mlp(nc, io, h, u_hi, u_lo, last)
        give_back(nc, io, h, last)


def bucket(d):
    half = 16
    far = half + (np.log(np.maximum(d, 1).astype(np.float32) / np.float32(half)) / np.float32(math.log(2048 / half))
                  * np.float32(half)).astype(np.int32)
    return np.where(d < half, d, np.minimum(far, 31))


def constants():
    out = {"ident": np.eye(P, dtype=np.float32)}
    dist = 2 * WIN - 1 - np.arange(LINE)
    seen = (dist >= 0) & (dist <= WIN)
    hot = np.zeros((33, 3, LINE), np.float32)
    for i, dil in enumerate(DILS):
        hot[32, i, ~seen] = NEG
        hot[bucket(dist[seen] * dil), i, np.flatnonzero(seen)] = 1.0
    out["hot"] = hot.reshape(33, 3 * LINE)
    t = np.arange(NS)
    same = (t[:, None] // DEC_T == t[None, :] // DEC_T)
    cross = np.where(same, 0.0, NEG)
    other = np.where(np.eye(NS) > 0, 0.0, NEG)
    out["masks_s"] = np.tile(np.stack([cross, other], axis=1), (4, 1, 1)).astype(np.float32)
    out["upper"] = np.triu(np.ones((P, P), np.float32))
    out["upper_s"] = (same & (t[:, None] <= t[None, :])).astype(np.float32)
    out["same_s"] = same.astype(np.float32)
    out["of_seq"] = (t[:, None] // DEC_T == np.arange(DEC_N)[None, :]).astype(np.float32)
    return out


def shaped_inputs(i):
    c = np.ascontiguousarray

    def by_channel(v):
        return c(np.moveaxis(v.reshape(-1, P, *v.shape[1:]), 0, 1))

    w = i["w_in"][0]
    w_in = np.concatenate([w[:, h * HD:(h + 1) * HD] for h in (0, 2, 1, 3)] + [w[:, 4 * HD:]], axis=1)
    out = {
        "x": c(np.concatenate([i["x_prompt"][0], i["x_sample"].reshape(NS, D)])),
        "norm_mix_g": by_channel(i["norm_mix_g"][0]), "w_in": w_in,
        "a_q_norm_g": c(i["a_q_norm_g"][0]), "a_k_norm_g": c(i["a_k_norm_g"][0]),
        "c_q_norm_g": c(i["c_q_norm_g"][0]), "c_k_norm_g": c(i["c_k_norm_g"][0]),
        "conv_w": by_channel(i["conv_w"][0].T), "conv_b": by_channel(i["conv_b"][0]),
        "state_conv": by_channel(i["state_conv"][0].transpose(2, 0, 1)),
    }
    out["d_skip"] = by_channel(np.repeat(i["d_skip"][0], HD))
    out["ssm_norm_g"] = by_channel(i["ssm_norm_g"][0])
    out["dt_bias"], out["a_log"] = c(i["dt_bias"][0]), c(i["a_log"][0])
    out["state_ssm"] = c(i["state_ssm"][0].transpose(3, 0, 1, 2).reshape(STATE, DEC_N, 512))
    out["norm_mlp_g"] = by_channel(i["norm_mlp_g"][0])
    out["w_out"], out["w_up"], out["w_down"] = (c(i[s][0]) for s in ("w_out", "w_up", "w_down"))
    out["rel_bias"] = c(i["rel_bias"])
    out["a_sinks"] = c(i["a_sinks"][0])
    ak, av, ck, cv = (i[s][0] for s in ("cache_a_k", "cache_a_v", "cache_c_k", "cache_c_v"))
    blocks = [slice(2048 - WIN, 2048)] + [slice(2048 - WIN * dil + t, 2048, dil) for dil in DILS[1:] for t in range(DEC_T)]
    out["a_kt"] = c(ak.transpose(0, 3, 2, 1))
    out["a_v"] = c(av.reshape(DEC_N, WIN, P))
    out["c_kt"] = c(np.concatenate([ck[:, b] for b in blocks], axis=1).transpose(0, 3, 2, 1))
    out["c_v"] = c(np.stack([cv[:, b].reshape(DEC_N, WIN, 256) for b in blocks], axis=2).reshape(DEC_N, WIN, 9 * 256))
    return out


OUTS = {"y": (TOK, D), "tok": (TOK, TC), "p_conv": (P, KT, 3), "s_conv": (P, KT, DEC_N, 3), "p_ssm": (STATE, 512), "s_ssm": (STATE, DEC_N, 512)}
SCRATCH = {"zs": ((512, TOK), F32), "xc": ((D, TOK), F32), "mix_hi": ((D, TOK), F16), "mix_lo": ((D, TOK), F16),
           "lines": ((16, P, LINE), F32), "sums": ((4, SEQ, OROW), F32)}


def kernel(**inputs):
    import concourse.bacc as _bacc
    from concourse.bass_utils import run_bass_kernel_spmd as _run

    nc = _bacc.Bacc("TRN2", target_bir_lowering=False, num_devices=1)
    arrays = {**shaped_inputs({k: np.asarray(v) for k, v in inputs.items()}), **constants()}
    io = {k: nc.dram_tensor(f"in_{k}", v.shape, mybir.dt.from_np(v.dtype), kind="ExternalInput").ap() for k, v in arrays.items()}
    for k, shape in OUTS.items():
        io[k] = nc.dram_tensor(f"out_{k}", shape, F32, kind="ExternalOutput").ap()
    for k, (shape, dt) in SCRATCH.items():
        io[k] = nc.dram_tensor(f"scratch_{k}", shape, dt).ap()
    build(nc, io)
    r = _run(nc, [{f"in_{k}": v for k, v in arrays.items()}], core_ids=[0]).results[0]
    got = {k: r[f"out_{k}"] for k in OUTS}

    y, tok = got["y"], got["tok"]

    def heads(cols, rows, *lead):
        return np.ascontiguousarray(tok[rows, cols]).reshape(1, *lead, -1, HD)

    ak, av, ck, cv = slice(256, 384), slice(384, 512), slice(768, 1024), slice(1024, 1280)
    last, prompt, sample = slice(SEQ - WIN, SEQ), slice(0, SEQ), slice(SEQ, TOK)
    p_conv = got["p_conv"].transpose(2, 1, 0).reshape(1, 1, 3, D)
    s_conv = got["s_conv"].transpose(2, 3, 1, 0).reshape(1, DEC_N, 3, D)
    p_ssm = got["p_ssm"].T.reshape(1, 1, HB, HD, STATE)
    s_ssm = got["s_ssm"].transpose(1, 2, 0).reshape(1, DEC_N, HB, HD, STATE)
    c = np.ascontiguousarray
    return (c(y[:SEQ])[None], c(y[SEQ:]).reshape(DEC_N, DEC_T, D),
            heads(ak, last, 1, WIN), heads(av, last, 1, WIN), heads(ck, prompt, 1, SEQ), heads(cv, prompt, 1, SEQ), c(p_ssm), c(p_conv),
            heads(ak, sample, DEC_N, DEC_T), heads(av, sample, DEC_N, DEC_T), heads(ck, sample, DEC_N, DEC_T), heads(cv, sample, DEC_N, DEC_T),
            c(s_ssm), c(s_conv))
```
